# Optimizing a Trainium2 kernel written in Bass

```python
import jax, jax.numpy as jnp
from jax import lax
import numpy as np

D_MODEL = 1024
BATCH = 1
SEQ = 512
DEPTH = 1
DEC_BATCH = 1
DEC_SEQ = 64
PAST_LEN = 256

CHUNK = 64
Q_BLOCK = 128
N_MEM = 256
FOX_HEADS = 8
FOX_HEAD_DIM = 64
FOX_WIDTH = FOX_HEADS * FOX_HEAD_DIM
MLA_HEADS = 8
MLA_NOPE_DIM = 64
MLA_ROPE_DIM = 32
MLA_V_DIM = 64
MLA_WIDTH = MLA_HEADS * MLA_V_DIM
MLA_Q_RANK = 384
MLA_KV_RANK = 256
MIX_WIDTH = FOX_WIDTH + MLA_WIDTH
MEM_HEADS = 4
MEM_HEAD_DIM = 128
MEM_WIDTH = MEM_HEADS * MEM_HEAD_DIM
D_FF = -(-8 * D_MODEL // (3 * 256)) * 256
ROPE_THETA = 10000.0
RMS_EPS = 1e-6
FORGET_BIAS_INIT = 3.0
FOX_SCALE = FOX_HEAD_DIM ** -0.5
MLA_SCALE = (MLA_NOPE_DIM + MLA_ROPE_DIM) ** -0.5
MEM_SCALE = MEM_HEAD_DIM ** -0.5
IN_SPLITS = (FOX_WIDTH, FOX_WIDTH, FOX_WIDTH, FOX_HEADS, MLA_Q_RANK, MLA_KV_RANK, MLA_ROPE_DIM)
IN_WIDTH = 3 * FOX_WIDTH + FOX_HEADS + MLA_Q_RANK + MLA_KV_RANK + MLA_ROPE_DIM

kernel_name = "hybrid_fox_mla_streaming_step"

def rms_norm(x, g):
    xf = x.astype(jnp.float32)
    y = xf * lax.rsqrt(jnp.mean(xf * xf, axis=-1, keepdims=True) + RMS_EPS)
    return (y * g.astype(jnp.float32)).astype(x.dtype)

def rope_tables(pos):
    half = MLA_ROPE_DIM // 2
    inv = ROPE_THETA ** (-jnp.arange(half, dtype=jnp.float32) / half)
    ang = pos.astype(jnp.float32)[:, None] * inv[None, :]
    return jnp.cos(ang), jnp.sin(ang)

def apply_rope(x, cos, sin):
    xf = x.astype(jnp.float32)
    x1, x2 = jnp.split(xf, 2, axis=-1)
    return jnp.concatenate([x1 * cos - x2 * sin, x2 * cos + x1 * sin], axis=-1).astype(x.dtype)

def attend(q, k, v, q_pos, k_pos, scale, unit, q_bias=None, k_bias=None):
    s = jnp.einsum("bqhd,bkhd->bhqk", q, k).astype(jnp.float32) * scale
    if q_bias is not None:
        s = s + jnp.swapaxes(q_bias, 1, 2)[..., :, None] - jnp.swapaxes(k_bias, 1, 2)[..., None, :]
    visible = (k_pos[None, :] // unit) <= (q_pos[:, None] // unit)
    s = jnp.where(visible, s, -jnp.inf)
    p = jax.nn.softmax(s, axis=-1).astype(v.dtype)
    return jnp.einsum("bhqk,bkhd->bqhd", p, v)

def attend_blocks(q, k, v, q_pos, k_pos, scale, unit, q_bias=None, k_bias=None):
    B, T, H, dk = q.shape
    nb = T // Q_BLOCK
    qb = jnp.swapaxes(q.reshape(B, nb, Q_BLOCK, H, dk), 0, 1)
    pb = q_pos.reshape(nb, Q_BLOCK)
    if q_bias is None:
        out = lax.map(lambda a: attend(a[0], k, v, a[1], k_pos, scale, unit), (qb, pb))
    else:
        bb = jnp.swapaxes(q_bias.reshape(B, nb, Q_BLOCK, H), 0, 1)
        out = lax.map(lambda a: attend(a[0], k, v, a[1], k_pos, scale, unit, a[2], k_bias), (qb, pb, bb))
    return jnp.swapaxes(out, 0, 1).reshape(B, T, H, v.shape[-1])

def project_mixers(h, pos, w_in, b_f, g_cq, w_uq, g_ckv):
    B, T, _ = h.shape
    z = h @ w_in
    offs = np.cumsum(IN_SPLITS)[:-1].tolist()
    q_f, k_f, v_f, f_logit, c_q, c_kv, k_r = jnp.split(z, offs, axis=-1)
    fox_q = q_f.reshape(B, T, FOX_HEADS, FOX_HEAD_DIM)
    fox_k = k_f.reshape(B, T, FOX_HEADS, FOX_HEAD_DIM)
    fox_v = v_f.reshape(B, T, FOX_HEADS, FOX_HEAD_DIM)
    logf = jax.nn.log_sigmoid((f_logit + b_f).astype(jnp.float32))
    cos, sin = rope_tables(pos)
    q_m = (rms_norm(c_q, g_cq) @ w_uq).reshape(B, T, MLA_HEADS, MLA_NOPE_DIM + MLA_ROPE_DIM)
    q_nope, q_rope = jnp.split(q_m, [MLA_NOPE_DIM], axis=-1)
    mla_q = jnp.concatenate([q_nope, apply_rope(q_rope, cos[:, None, :], sin[:, None, :])], axis=-1)
    ckv = rms_norm(c_kv, g_ckv)
    kr = apply_rope(k_r, cos, sin)
    return fox_q, fox_k, fox_v, logf, mla_q, ckv, kr

def mla_keys_values(ckv, kr, w_ukv):
    B, S, _ = ckv.shape
    kv = (ckv @ w_ukv).reshape(B, S, MLA_HEADS, MLA_NOPE_DIM + MLA_V_DIM)
    k_nope, v = jnp.split(kv, [MLA_NOPE_DIM], axis=-1)
    k = jnp.concatenate([k_nope, jnp.broadcast_to(kr[:, :, None, :], (B, S, MLA_HEADS, MLA_ROPE_DIM))], axis=-1)
    return k, v

def memory_kv(mem, g_mem_src, w_mk, w_mv):
    B, M, _ = mem.shape
    m = rms_norm(mem, g_mem_src)
    return ((m @ w_mk).reshape(B, M, MEM_HEADS, MEM_HEAD_DIM),
            (m @ w_mv).reshape(B, M, MEM_HEADS, MEM_HEAD_DIM))

def trunk_layer(x, pos, mem_k, mem_v, past, w):
    (g_mix, w_in, b_f, g_cq, w_uq, g_ckv, w_ukv, g_fox_out, g_mla_out, w_o,
     g_mem, w_mq, w_mo, g_ffn, w_gate, w_up, w_down) = w
    B, T, _ = x.shape
    h = rms_norm(x, g_mix)
    fox_q, fox_k, fox_v, logf, mla_q, ckv, kr = project_mixers(h, pos, w_in, b_f, g_cq, w_uq, g_ckv)
    if past is None:
        cum = jnp.cumsum(logf, axis=1)
        fox_o = attend_blocks(fox_q, fox_k, fox_v, pos, pos, FOX_SCALE, 1, cum, cum)
        mk, mv = mla_keys_values(ckv, kr, w_ukv)
        mla_o = attend_blocks(mla_q, mk, mv, pos, pos, MLA_SCALE, CHUNK)
    else:
        c_fk, c_fv, c_lf, c_ckv, c_kr = past
        P = c_fk.shape[1]
        k_pos = jnp.arange(P + T, dtype=jnp.int32)
        cum = jnp.cumsum(jnp.concatenate([c_lf.astype(jnp.float32), logf], axis=1), axis=1)
        fox_o = attend(fox_q, jnp.concatenate([c_fk, fox_k], axis=1), jnp.concatenate([c_fv, fox_v], axis=1),
                       pos, k_pos, FOX_SCALE, 1, cum[:, P:], cum)
        mk, mv = mla_keys_values(jnp.concatenate([c_ckv, ckv], axis=1), jnp.concatenate([c_kr, kr], axis=1), w_ukv)
        mla_o = attend(mla_q, mk, mv, pos, k_pos, MLA_SCALE, CHUNK)
    mixed = jnp.concatenate([rms_norm(fox_o.reshape(B, T, FOX_WIDTH), g_fox_out),
                             rms_norm(mla_o.reshape(B, T, MLA_WIDTH), g_mla_out)], axis=-1)
    x = x + mixed @ w_o
    q = (rms_norm(x, g_mem) @ w_mq).reshape(B, T, MEM_HEADS, MEM_HEAD_DIM)
    s = jnp.einsum("bqhd,bmhd->bhqm", q, mem_k).astype(jnp.float32) * MEM_SCALE
    p = jax.nn.softmax(s, axis=-1).astype(mem_v.dtype)
    o = jnp.einsum("bhqm,bmhd->bqhd", p, mem_v).reshape(B, T, MEM_WIDTH)
    x = x + o @ w_mo
    hf = rms_norm(x, g_ffn)
    x = x + (jax.nn.silu(hf @ w_gate) * (hf @ w_up)) @ w_down
    return x, (fox_k, fox_v, logf, ckv, kr)

def setup_inputs(seed: int = 0) -> dict:
    key = jax.random.key(seed)
    ks = iter(jax.random.split(key, 40))
    f32 = jnp.float32

    def nrm(shape, scale=1.0):
        return jax.random.normal(next(ks), shape, f32) * scale

    def gain(n):
        return 1.0 + nrm((DEPTH, n), 0.02)

    L = DEPTH
    return {
        "x_prompt": nrm((BATCH, SEQ, D_MODEL)),
        "x_sample": nrm((DEC_BATCH, DEC_SEQ, D_MODEL)),
        "mem_prompt": nrm((BATCH, N_MEM, D_MODEL)),
        "cache_fox_k": nrm((L, DEC_BATCH, PAST_LEN, FOX_HEADS, FOX_HEAD_DIM)),
        "cache_fox_v": nrm((L, DEC_BATCH, PAST_LEN, FOX_HEADS, FOX_HEAD_DIM)),
        "cache_fox_logf": jax.nn.log_sigmoid(FORGET_BIAS_INIT + nrm((L, DEC_BATCH, PAST_LEN, FOX_HEADS))),
        "cache_mla_ckv": nrm((L, DEC_BATCH, PAST_LEN, MLA_KV_RANK)),
        "cache_mla_kr": nrm((L, DEC_BATCH, PAST_LEN, MLA_ROPE_DIM)),
        "cache_mem_k": nrm((L, DEC_BATCH, N_MEM, MEM_HEADS, MEM_HEAD_DIM)),
        "cache_mem_v": nrm((L, DEC_BATCH, N_MEM, MEM_HEADS, MEM_HEAD_DIM)),
        "g_mix": gain(D_MODEL),
        "w_in": nrm((L, D_MODEL, IN_WIDTH), D_MODEL ** -0.5),
        "b_f": FORGET_BIAS_INIT + nrm((L, FOX_HEADS), 0.1),
        "g_cq": gain(MLA_Q_RANK),
        "w_uq": nrm((L, MLA_Q_RANK, MLA_HEADS * (MLA_NOPE_DIM + MLA_ROPE_DIM)), MLA_Q_RANK ** -0.5),
        "g_ckv": gain(MLA_KV_RANK),
        "w_ukv": nrm((L, MLA_KV_RANK, MLA_HEADS * (MLA_NOPE_DIM + MLA_V_DIM)), MLA_KV_RANK ** -0.5),
        "g_fox_out": gain(FOX_WIDTH),
        "g_mla_out": gain(MLA_WIDTH),
        "w_o": nrm((L, MIX_WIDTH, D_MODEL), MIX_WIDTH ** -0.5),
        "g_mem_src": gain(D_MODEL),
        "w_mk": nrm((L, D_MODEL, MEM_WIDTH), D_MODEL ** -0.5),
        "w_mv": nrm((L, D_MODEL, MEM_WIDTH), D_MODEL ** -0.5),
        "g_mem": gain(D_MODEL),
        "w_mq": nrm((L, D_MODEL, MEM_WIDTH), D_MODEL ** -0.5),
        "w_mo": nrm((L, MEM_WIDTH, D_MODEL), MEM_WIDTH ** -0.5),
        "g_ffn": gain(D_MODEL),
        "w_gate": nrm((L, D_MODEL, D_FF), D_MODEL ** -0.5),
        "w_up": nrm((L, D_MODEL, D_FF), D_MODEL ** -0.5),
        "w_down": nrm((L, D_FF, D_MODEL), D_FF ** -0.5),
        "g_final": 1.0 + nrm((D_MODEL,), 0.02),
    }

def reference(x_prompt, x_sample, mem_prompt, cache_fox_k, cache_fox_v, cache_fox_logf,
              cache_mla_ckv, cache_mla_kr, cache_mem_k, cache_mem_v,
              g_mix, w_in, b_f, g_cq, w_uq, g_ckv, w_ukv, g_fox_out, g_mla_out, w_o,
              g_mem_src, w_mk, w_mv, g_mem, w_mq, w_mo, g_ffn, w_gate, w_up, w_down, g_final):
    t_p = x_prompt.shape[1]
    t_s = x_sample.shape[1]
    past_len = cache_fox_k.shape[2]
    pos_p = jnp.arange(t_p, dtype=jnp.int32)
    pos_s = past_len + jnp.arange(t_s, dtype=jnp.int32)
    xp, xs = x_prompt, x_sample
    rows_p, rows_s, mem_p = [], [], []
    for l in range(DEPTH):
        w = (g_mix[l], w_in[l], b_f[l], g_cq[l], w_uq[l], g_ckv[l], w_ukv[l], g_fox_out[l], g_mla_out[l], w_o[l],
             g_mem[l], w_mq[l], w_mo[l], g_ffn[l], w_gate[l], w_up[l], w_down[l])
        mk_p, mv_p = memory_kv(mem_prompt, g_mem_src[l], w_mk[l], w_mv[l])
        xp, rp = trunk_layer(xp, pos_p, mk_p, mv_p, None, w)
        past = (cache_fox_k[l], cache_fox_v[l], cache_fox_logf[l], cache_mla_ckv[l], cache_mla_kr[l])
        xs, rs = trunk_layer(xs, pos_s, cache_mem_k[l], cache_mem_v[l], past, w)
        rows_p.append(rp)
        rows_s.append(rs)
        mem_p.append((mk_p, mv_p))
    y_prompt = rms_norm(xp, g_final)
    y_sample = rms_norm(xs, g_final)
    p_fox_k = jnp.stack([r[0] for r in rows_p])
    p_fox_v = jnp.stack([r[1] for r in rows_p])
    p_fox_logf = jnp.stack([r[2] for r in rows_p])
    p_mla_ckv = jnp.stack([r[3] for r in rows_p])
    p_mla_kr = jnp.stack([r[4] for r in rows_p])
    p_mem_k = jnp.stack([m[0] for m in mem_p])
    p_mem_v = jnp.stack([m[1] for m in mem_p])
    s_fox_k = jnp.stack([r[0] for r in rows_s])
    s_fox_v = jnp.stack([r[1] for r in rows_s])
    s_fox_logf = jnp.stack([r[2] for r in rows_s])
    s_mla_ckv = jnp.stack([r[3] for r in rows_s])
    s_mla_kr = jnp.stack([r[4] for r in rows_s])
    return (y_prompt, y_sample, p_fox_k, p_fox_v, p_fox_logf, p_mla_ckv, p_mla_kr, p_mem_k, p_mem_v,
            s_fox_k, s_fox_v, s_fox_logf, s_mla_ckv, s_mla_kr)


_drawn_inputs = setup_inputs


def setup_inputs(seed=0):
    import zlib

    import numpy as np

    out = dict(_drawn_inputs(seed))
    spreads = {}
    factors = {'g_cq': 5.288,
     'g_ckv': 3.034,
     'g_fox_out': 5.478,
     'g_mla_out': 5.395,
     'g_mem_src': 2.948,
     'g_mem': 8.0,
     'g_ffn': 5.029,
     'g_final': 7.551,
     'cache_mla_ckv': 8.0,
     'cache_mla_kr': 4.365}
    for name, (base, spread) in spreads.items():
        noise = np.random.default_rng([zlib.crc32(name.encode()), seed]).standard_normal(out[name].shape)
        drawn = base * np.exp(spread * noise) if base else spread * noise
        out[name] = __import__('jax').numpy.asarray(drawn.astype(out[name].dtype))
    for name, factor in factors.items():
        out[name] = (out[name] * factor).astype(out[name].dtype)
    return out
```

```python
from contextlib import ExitStack

import numpy as np

import concourse.bass as bass
from concourse import mybir

F32 = mybir.dt.float32
F32R = mybir.dt.float32r
BF16 = mybir.dt.bfloat16
ALU = mybir.AluOpType
ACT = mybir.ActivationFunctionType
AX = mybir.AxisListType.X

D = 1024
TP, TS = 512, 64
T = TP + TS
HT = T // 2
PAST = 256
NK = TP + PAST + TS
H, HD = 8, 64
QR, KVR, RD = 384, 256, 32
NM, MH, MD = 256, 4, 128
FF = 2816
KT = D // 128
FT = FF // 128
TT = 5
WB = 1024
SLOTS = 4
RAWS = 2
FOX_SCALE = HD ** -0.5
MLA_SCALE = (HD + RD) ** -0.5
MEM_SCALE = MD ** -0.5
EPS = 1e-6
BIG = 3.0e38
MASKED = -1.0e30
IN_W = 3 * H * HD + H + QR + KVR + RD
TAIL0 = 3 * H * HD
TAIL_W = IN_W - TAIL0
TG = TAIL_W // 2

B_QK = 0
B_V = B_QK + 8
B_TAIL = B_V + 4
B_UQ = B_TAIL + 8
B_UKV = B_UQ + 4
B_WO = B_UKV + 2
B_MKV = B_WO + 8
B_MQ = B_MKV + 8
B_MO = B_MQ + 4
B_FF = B_MO + 8
B_DOWN = B_FF + 2 * FT
B_END = B_DOWN + 32
DOWN_K = (6, 6, 5, 5)

C_ID, C_CAUSAL, C_CHUNK, C_TRI = 0, 128, 256, 384
C_ROPE = C_TRI + 512
C_COS = C_ROPE + T
C_SIN = C_COS + TT * 16
C_END = C_SIN + TT * 16


def tok(tt):
    return 128 if tt < 4 else TS


def build(nc, i_, o_, cum_dram):
    end = nc.sbuf_usable_end
    cursor = (nc.sbuf_base + 63) // 64 * 64

    def place(name, shape, dt, at):
        size = int(np.prod(shape[1:])) * (2 if dt == BF16 else 4)
        assert at + size <= end, (name, at, size, end)
        return nc.alloc_sbuf_tensor_at(name, list(shape), dt, offset=at), at + (size + 63) // 64 * 64

    xT, cursor = place("xT", [128, KT, T], F32, cursor)
    wraw, cursor = place("wraw", [128, RAWS, WB], F32, cursor)
    whi, cursor = place("whi", [128, SLOTS, WB], F32R, cursor)
    wlo, cursor = place("wlo", [128, SLOTS, WB], F32R, cursor)
    ident, cursor = place("ident", [128, 128], F32, cursor)
    rstd, cursor = place("rstd", [128, T], F32, cursor)
    rcol, cursor = place("rcol", [128, 8], F32, cursor)
    gains, cursor = place("gains", [128, 64], F32, cursor)
    small, cursor = place("small", [128, 64], F32, cursor)
    sqacc, cursor = place("sqacc", [128, T], F32, cursor)
    ones, cursor = place("ones", [128, 128], F32, cursor)
    tmp2, cursor = place("tmp2", [128, 2, T], F32, cursor)
    hbase = cursor
    hhi, cursor = place("hhi", [128, KT, T], F32R, hbase)
    hlo, cursor = place("hlo", [128, KT, T], F32R, cursor)
    vbase = cursor
    hidhi, c = place("hidhi", [128, FT, T], F32R, vbase)
    hidlo, c = place("hidlo", [128, FT, T], F32R, c)
    yg, c = place("yg", [128, KT, T], F32, hbase)
    yout, c = place("yout", [128, 2, D], F32, c)

    qraw, c = place("qraw", [128, 4, T], F32, vbase)
    kraw, c = place("kraw", [128, 4, NK], F32, c)
    vraw, c = place("vraw", [128, 7, H * HD], F32, c)
    aslot = c
    nat, c = place("nat", [128, TT, TAIL_W], F32, aslot)
    xn, _ = place("xn", [128, TT, D], F32, aslot)
    pthi_f, c = place("pthi_f", [128, 13 * 128 + 192], F32R, aslot)
    ptlo_f, c = place("ptlo_f", [128, 13 * 128 + 192], F32R, c)
    bslot = c
    cqT, c = place("cqT", [128, 3, T], F32, bslot)
    ckvT, c = place("ckvT", [128, 2, NK], F32, c)
    pthi_m, c2 = place("pthi_m", [128, 13 * 128 + 192], F32R, bslot)
    ptlo_m, c2 = place("ptlo_m", [128, 13 * 128 + 192], F32R, c2)
    c = max(c, c2)
    ncum, _ = place("ncum", [8, NK], F32, c)
    probs, c = place("probs", [128, 5, 512], F32, c)
    krT, c = place("krT", [128, NK], F32, c)
    oT, cend = place("oT", [128, 8, T], F32, c)
    tri, c2 = place("tri", [128, 512], F32, c)
    cosn, c2 = place("cosn", [128, TT, 16], F32, c2)
    sinn, c2 = place("sinn", [128, TT, 16], F32, c2)
    gckv, c2 = place("gckv", [128, KVR], F32, c2)
    cckv, c2 = place("cckv", [128, 2, KVR], F32, c2)
    ckn, c2 = place("ckn", [128, 2, H * HD], F32, c2)
    ckr, c2 = place("ckr", [128, 2, RD], F32, c2)
    ropt, c2 = place("ropt", [128, 160], F32, c2)
    assert c2 <= cend
    maskb, c = place("maskb", [128, 2, 128], BF16, cend)
    identb, c = place("identb", [128, 128], BF16, c)
    rope, c = place("rope", [128, T], F32, c)
    osum, c = place("osum", [64, T], F32, c)
    maskf, c = place("maskf", [128, 2, 128], F32, c)
    kout, _ = place("kout", [128, 2, H * HD], F32, bslot + 13696)
    kh, c = place("kh", [128, 2, NK], F32R, hbase)
    kl, c = place("kl", [128, 2, NK], F32R, c)
    ckv_base = hbase + 2 * 3 * T * 4
    assert c <= ckv_base
    vh, c = place("vh", [128, 2, 7, 128], F32R, ckv_base)
    nck, c = place("nck", [128, 2, NK], F32, c)
    qh, c = place("qh", [128, 2, T], F32R, c)
    ql, c = place("ql", [128, 2, T], F32R, c)
    assert c <= vbase
    qm, c = place("qm", [128, H, T], F32, vbase)
    km, c = place("km", [128, 4, NK], F32, c)
    vm, c = place("vm", [128, 7, H * HD], F32, c)
    assert c <= bslot
    cqhi, c = place("cqhi", [128, 3, T], F32R, hbase)
    cqlo, c = place("cqlo", [128, 3, T], F32R, c)
    assert c == ckv_base
    ckvhi, c = place("ckvhi", [128, 2, NK], F32R, c)
    ckvlo, c = place("ckvlo", [128, 2, NK], F32R, c)
    assert c <= ckv_base + 2 * 7 * 128 * 4 + 2 * NK * 4
    memT_h, c = place("memT_h", [128, KT, NM], F32R, vbase)
    memT_l, c = place("memT_l", [128, KT, NM], F32R, c)
    memn, c = place("memn", [128, 2, D], F32, c)
    qmh, c1 = place("qmh", [128, 2, T], F32R, vbase)
    qml, c1 = place("qml", [128, 2, T], F32R, c1)
    kmh, c1 = place("kmh", [128, 2, 512], F32R, c1)
    kml, c1 = place("kml", [128, 2, 512], F32R, c1)
    vmh, c1 = place("vmh", [128, 2, 4, 128], F32R, c1)
    vml, c1 = place("vml", [128, 2, 4, 128], F32R, c1)
    c = max(c, c1)
    memv, c = place("memv", [128, 4, 512], F32, c)
    memk, c = place("memk", [128, 4, 512], F32, c)
    mkT, c = place("mkT", [128, MH, 512], F32, c)
    mqT, c = place("mqT", [128, MH, T], F32, c)
    mpth, c = place("mpth", [128, 2 * 512 + 128], F32R, c)
    mptl, c = place("mptl", [128, 2 * 512 + 128], F32R, c)
    mprobs, c = place("mprobs", [128, 5, 256], F32, c)
    assert c <= end
    mohi, c = place("mohi", [128, MH, T], F32R, hbase)
    molo, c = place("molo", [128, MH, T], F32R, c)

    with ExitStack() as ctx:
        ps = ctx.enter_context(nc.psum_tensor("ps", [128, 8, 512], F32))
        flat = ps[:, :, :].rearrange("p a b -> p (a b)")
        sems = {}

        def sem(name):
            if name not in sems:
                sems[name] = ctx.enter_context(nc.semaphore(name))
            return sems[name]

        def two(pair):
            return ps[:, 2 * pair:2 * pair + 2, 0:HT]

        def halves(ap):
            return ap.rearrange("p (a b) -> p a b", a=2)

        G_MIX, G_CQ, G_OUT, G_MEM, G_FFN, G_FIN, G_SRC = 0, 8, 11, 19, 27, 35, 43
        S_BF, S_SUM, S_NMAX, S_RINV, S_SS, S_CLF, S_EPS, S_WAIT = 0, 8, 13, 18, 24, 36, 60, 52


        w_load = [sem("w_loaded0"), sem("w_loaded1")]
        w_hi, w_lo = sem("w_hi"), sem("w_lo")
        w_used = sem("w_used")
        s_in, s_in2, s_memin = sem("s_in"), sem("s_in2"), sem("s_memin")
        s_const, s_tx, s_x = sem("s_const"), sem("s_tx"), sem("s_x")
        s_hhi, s_hlo = sem("s_hhi"), sem("s_hlo")
        s_sq, s_acc, s_ms = sem("s_sq"), sem("s_acc"), sem("s_ms")
        s_std, s_rstd = sem("s_std"), sem("s_rstd")
        s_ev = sem("s_ev")
        s_rt, s_rcol = sem("s_rt"), sem("s_rcol")
        s_vev, s_kt, s_kout, s_kdma = sem("s_vev"), sem("s_kt"), sem("s_kout"), [sem("s_kdma0"), sem("s_kdma1")]
        s_tail, s_z, s_lnf, s_logf = sem("s_tail"), sem("s_z"), sem("s_lnf"), sem("s_logf")
        s_ss, s_sstd, s_srstd = sem("s_ss"), sem("s_sstd"), sem("s_srstd")
        s_natn, s_kr1, s_kr2, s_kr3 = sem("s_natn"), sem("s_kr1"), sem("s_kr2"), sem("s_kr3")
        s_cum, s_ncum, s_cumd, s_nck = sem("s_cum"), sem("s_ncum"), sem("s_cumd"), [sem("s_nck0"), sem("s_nck1")]
        s_tc, s_tcev = sem("s_tc"), sem("s_tcev")
        s_krl = sem("s_krl")
        s_zero, s_vz, s_out = sem("s_zero"), sem("s_vz"), sem("s_out")
        s_chi, s_clo = sem("s_chi"), sem("s_clo")
        s_qcp, s_qr = sem("s_qcp"), sem("s_qr")
        s_vmev, s_qrope = sem("s_vmev"), sem("s_qrope")
        s_krp = sem("s_krp")
        s_onorm = sem("s_onorm")
        s_mss, s_mstd, s_mrstd = sem("s_mss"), sem("s_mstd"), sem("s_mrstd")
        s_mt, s_mth, s_mtl = sem("s_mt"), sem("s_mth"), sem("s_mtl")
        s_mkv, s_mkt, s_mktev = sem("s_mkv"), sem("s_mkt"), sem("s_mktev")
        s_silu, s_gr, s_h2, s_hf, s_hidhi, s_hidlo = (sem("s_silu"), sem("s_gr"), sem("s_h2"), sem("s_hf"), sem("s_hidhi"),
                                                        sem("s_hidlo"))
        s_yg, s_yt, s_yev, s_ydma = sem("s_yg"), sem("s_yt"), sem("s_yev"), [sem("s_ydma0"), sem("s_ydma1")]

        def dmas(b):
            return 7 if B_UQ <= b < B_UKV else 4 if B_UKV <= b < B_WO else 1

        def loaded(b):
            return 16 * sum(dmas(x) for x in range(b % RAWS, b + 1, RAWS))

        NORMS = dict(mix=8, fox=4, mla=4, mem=8, ffn=8, fin=8)
        sq0, acc0, nth = {}, {}, {}
        for k, name in enumerate(NORMS):
            before = list(NORMS.values())[:k]
            nth[name], sq0[name], acc0[name] = k, sum(before), sum(before) + k

        E_QK, E_UQ, E_UKV, E_WO, E_MQ, E_MO, E_DOWN = 0, 8, 16, 20, 28, 32, 40
        N_MIX, N_OUT, N_MEM, N_FFN = 0, 8, 16, 24

        def wv(b, lo, k, n):
            t = wlo if lo else whi
            return t[:, b % SLOTS, 0:k * n].rearrange("p (k n) -> p k n", k=k)

        SCORE_BANK, TURN_BANK = (0, 1, 2, 0, 1), (3, 4, 7, 3, 4)

        class Attn:

            def __init__(self, name, heads):
                self.name, self.heads = name, heads
                self.mem = name == "mem"
                self.prep_a, self.prep_p = sem(f"{name}_prep_a"), sem(f"{name}_prep_p")
                self.prep_va, self.prep_vp = sem(f"{name}_prep_va"), sem(f"{name}_prep_vp")
                self.pv0 = sem(f"{name}_pv0")
                self.qk = sem(f"{name}_qk")
                self.mx, self.ex = sem(f"{name}_mx"), sem(f"{name}_ex")
                self.ri, self.pn = sem(f"{name}_ri"), sem(f"{name}_pn")
                self.tr = sem(f"{name}_tr")
                self.pthi, self.ptlo = sem(f"{name}_pthi"), sem(f"{name}_ptlo")
                self.pv, self.oc, self.o = sem(f"{name}_pv"), sem(f"{name}_oc"), sem(f"{name}_o")
                if name == "fox":
                    self.pthi_t, self.ptlo_t, self.q, self.k, self.v, self.o0 = pthi_f, ptlo_f, qraw, kraw, vraw, 0
                if name == "mla":
                    self.pthi_t, self.ptlo_t, self.q, self.k, self.v, self.o0 = pthi_m, ptlo_m, qm, km, vm, 4
                if self.mem:
                    self.pthi_t, self.ptlo_t, self.q, self.k, self.v = mpth, mptl, mqT, mkT, memv
                self.p = mprobs if self.mem else probs
                self.sfree = self.mx if name == "fox" else self.ex

            def cols(self, u):
                if self.mem:
                    return NM
                return 128 * (u + 1) if u < 4 else PAST + TS

            def rows(self, u):
                return tok(u)

            def before(self, s):
                return s + 1 - (2, 2, 5, 3, 3)[s % 5]

            def score(self, s):
                u = s % 5
                return ps[0:self.rows(u), SCORE_BANK[u], 0:self.cols(u)]

            def blocks(self, u):
                return 2 if self.mem else (u + 1 if u < 4 else 3)

            def turned(self, s):
                u = s % 5
                return ps[:, TURN_BANK[u], 0:self.blocks(u) * 128].rearrange("p (b q) -> p b q", q=128)[:, :, 0:self.rows(u)]

            def kept(self, t, u):
                n = self.blocks(u)
                if self.mem:
                    if u == 4:
                        return t[:, 1024:1152].rearrange("p (b q) -> p b q", q=TS)
                    return t[:, 0:1024].rearrange("p (b q) -> p b q", q=512)[:, :, 128 * u:128 * u + 128]
                if u == 4:
                    return t[:, 13 * 128:13 * 128 + 192].rearrange("p (b q) -> p b q", q=TS)
                at, skip = (128, 256) if u == 3 else (128 * u, 0)
                return t[:, at:at + 384 * n].rearrange("p (b q) -> p b q", q=384)[:, :, skip:skip + 128]

        FOX, MLA, MEM = Attn("fox", H), Attn("mla", H), Attn("mem", MH)

        def need(eng, s, value, i=0, per=0):
            if isinstance(i, int):
                if value + per * i > 0:
                    eng.wait_ge(s, value + per * i)
            else:
                eng.wait_ge(s, i * per + value)

        small_loads = [
            (ckn[:, :, :], i_["cache_fox_k"].rearrange("(t p) n -> p t n", p=128)),
            (vraw[:, 4:6, :], i_["cache_fox_v"].rearrange("(t p) n -> p t n", p=128)),
            (small[:, S_CLF:S_CLF + 16].rearrange("p (t h) -> p t h", h=H), i_["cache_fox_logf"].rearrange("(t p) n -> p t n", p=128)),
            (cckv[:, :, :], i_["cache_mla_ckv"].rearrange("(t p) n -> p t n", p=128)),
            (ckr[:, :, :], i_["cache_mla_kr"].rearrange("(t p) n -> p t n", p=128)),
            (small[:, S_BF:S_BF + H], i_["b_f"].to_broadcast([128, H])),
            (gckv[:, :], i_["g_ckv"].to_broadcast([128, KVR])),
            (tri[:, :], i_["consts"][:, C_TRI:C_TRI + 512]),
            (rope[:, :], i_["consts"][:, C_ROPE:C_ROPE + T]),
            (cosn[:, :, :], i_["consts"][:, C_COS:C_SIN].rearrange("p (t c) -> p t c", t=TT)),
            (sinn[:, :, :], i_["consts"][:, C_SIN:C_END].rearrange("p (t c) -> p t c", t=TT)),
            (maskf[:, :, :], i_["consts"][:, C_CAUSAL:C_TRI].rearrange("p (t c) -> p t c", t=2)),
        ]
        N_IN2 = len(small_loads)
        first_loads = [
            (ident[:, :], i_["consts"][:, C_ID:C_ID + 128]),
            (xn[:, 0:4, :], i_["x_prompt"].rearrange("(t p) n -> p t n", p=128)),
            (xn[0:TS, 4, :], i_["x_sample"]),
        ] + [(gains[:, c:c + i_[g].shape[0] // 128], i_[g].rearrange("(k p) o -> p (k o)", p=128)) for g, c in (
            ("g_mix", G_MIX), ("g_cq", G_CQ), ("g_fox_out", G_OUT), ("g_mla_out", G_OUT + 4), ("g_mem", G_MEM),
            ("g_ffn", G_FFN), ("g_final", G_FIN), ("g_mem_src", G_SRC))]
        N_IN = len(first_loads)

        N_OUT_NAT, N_OUT_ALL = 8, 10

        block = ctx.enter_context(nc.Block())

        @block.tensor
        def _(pe):
            def product(out, b, pairs, start, stop):
                (lh, ll), (rh, rl) = pairs
                nc.tensor.matmul(out, lh, rh, start=start, stop=False)
                nc.tensor.matmul(out, ll, rh, start=False, stop=False)
                return nc.tensor.matmul(out, lh, rl, start=False, stop=stop)

            def a_block(b, kn, k0, xh, xl, pair, first, last, wait_k=None, weights=None, mean=None):
                for k in range(kn):
                    if mean and k == 4:
                        mean_square(mean)
                    if wait_k is not None:
                        pe.wait_ge(s_hlo, wait_k + k + 1)
                    for half in range(2):
                        cols = slice(half * HT, half * HT + HT)
                        w = (weights or (lambda lo, k: wv(b, lo, kn, 128)[:, k, :]))
                        mm = product(ps[:, 2 * pair + half, 0:HT], b, ((w(0, k), w(1, k)),
                                     (xh[:, k0 + k, cols], xl[:, k0 + k, cols])),
                                     first and k == 0, last and k == kn - 1)
                return mm

            def mean_square(name):
                pe.wait_ge(s_acc, acc0[name] + 1 + NORMS[name])
                for half in range(2):
                    mm = nc.tensor.matmul(ps[:, 6 + half, 0:HT], ones[:, :], sqacc[:, half * HT:half * HT + HT],
                                          start=True, stop=True)
                mm.then_inc(s_ms, 1)

            pe.wait_ge(s_in, 16 * N_IN)
            for j in range(KT):
                if j >= 2:
                    pe.wait_ge(s_x, j - 1)
                for tt in range(TT):
                    n = tok(tt)
                    mm = nc.tensor.transpose(flat[:, 1024 * (j % 2) + 128 * tt:1024 * (j % 2) + 128 * tt + n],
                                             xn[0:n, tt, 128 * j:128 * j + 128], ident[0:n, 0:n])
                mm.then_inc(s_tx, 1)

            def qk_body(i, first):
                for c in range(4):
                    b = B_QK + c
                    need(pe, w_lo, b + 1, i, 4)
                    need(pe, s_ev, E_QK + c - 1, i, 4)
                    a_block(b, KT, 0, hhi, hlo, c % 2, True, True,
                            N_MIX if first and c == 0 else None).then_inc(w_used, 1)
                    if first and c == 1:
                        mean_square("mix")

            pe.wait_ge(s_x, KT)
            qk_body(0, True)
            with pe.Fori(1, 2) as i:
                qk_body(i, False)
            pe.wait_ge(s_rstd, nth["mix"] + 1)
            for tt in range(TT):
                mm = nc.tensor.transpose(ps[0:tok(tt), 7, 32 * tt:32 * tt + 32],
                                         rstd[0:32, 128 * tt:128 * tt + tok(tt)], ident[0:32, 0:32])
            mm.then_inc(s_rt, 1)

            def b_block(b, kn, k0, width, banks, xh, xl, cols, first, last):
                for k in range(kn):
                    for tt, bank in enumerate(banks):
                        a, n = cols(tt)
                        mm = product(ps[0:n, bank, 0:width], b,
                                     ((xh[:, k0 + k, a:a + n], xl[:, k0 + k, a:a + n]),
                                      (wv(b, 0, kn, width)[:, k, :], wv(b, 1, kn, width)[:, k, :])),
                                     first and k == 0, last and k == kn - 1)
                return mm

            tokens = lambda tt: (128 * tt, tok(tt))
            pe.wait_ge(s_ev, E_QK + 8)
            for c in range(4):
                pe.wait_ge(w_lo, B_V + c + 1)
                b_block(B_V + c, 2, 2 * c, 512, range(TT), hhi, hlo, tokens, c == 0, c == 3).then_inc(w_used, 1)
            for tt in range(TT):
                if tt >= 2:
                    pe.wait_ge(s_kout, tt - 1)
                n, a = tok(tt), 128 * tt if tt < 4 else TP + PAST
                for p in range(4):
                    mm = nc.tensor.transpose(ps[0:n, 5 + tt % 2, 128 * p:128 * p + 128], kraw[:, p, a:a + n], ident[:, :])
                mm.then_inc(s_kt, 1)
            for g in range(2):
                pe.wait_ge(s_vev, TT) if g == 0 else pe.wait_ge(s_tail, TT)
                for c in range(4):
                    b = B_TAIL + 4 * g + c
                    pe.wait_ge(w_lo, b + 1)
                    b_block(b, 2, 2 * c, TG, range(TT), hhi, hlo, tokens, c == 0, c == 3).then_inc(w_used, 1)

            pe.wait_ge(s_kout, TT)
            pe.wait_ge(s_logf, 1)
            pe.wait_ge(s_in2, 16 * N_IN2)
            lf = ropt[:, 120:160].rearrange("p (t h) -> p t h", h=H)
            clf = small[:, S_CLF:S_CLF + 16].rearrange("p (t h) -> p t h", h=H)
            for t in range(4):
                nc.tensor.matmul(ps[0:8, 5, 128 * t:512], lf[:, t, :], tri[:, 0:512 - 128 * t],
                                 start=(t == 0), stop=(t == 3))
            nc.tensor.matmul(ps[0:8, 6, 0:320], clf[:, 0, :], tri[:, 0:320], start=True, stop=False)
            nc.tensor.matmul(ps[0:8, 6, 128:320], clf[:, 1, :], tri[:, 0:192], start=False, stop=False)
            nc.tensor.matmul(ps[0:8, 6, 256:320], lf[0:TS, 4, :], tri[0:TS, 0:TS],
                             start=False, stop=True).then_inc(s_cum, 1)
            pe.wait_ge(s_tail, 2 * TT)
            for p in range(4):
                for t in range(2):
                    mm = nc.tensor.transpose(flat[:, 256 * p + 128 * t:256 * p + 128 * t + 128],
                                             ckn[:, t, 128 * p:128 * p + 128], ident[:, :])
            mm.then_inc(s_tc, 1)
            pe.wait_ge(s_natn, 3)
            for j in range(3):
                at = 1024 * ((j + 1) % 2)
                if j >= 1:
                    pe.wait_ge(s_tcev, j)
                for tt in range(TT):
                    n = tok(tt)
                    mm = nc.tensor.transpose(flat[:, at + 128 * tt:at + 128 * tt + n],
                                             nat[0:n, tt, H + 128 * j:H + 128 * j + 128], ident[0:n, 0:n])
                mm.then_inc(s_tc, 1)
            for j in range(3):
                at = 1024 * (j % 2)
                pe.wait_ge(s_tcev, 3 + j)
                c0, w = (H + QR + 128 * j, 128) if j < 2 else (H + QR + KVR, RD)
                for tt in range(4):
                    nc.tensor.transpose(flat[0:w, at + 128 * tt:at + 128 * tt + 128], nat[:, tt, c0:c0 + w], ident[:, :])
                for t in range(2):
                    cached = cckv[:, t, 128 * j:128 * j + 128] if j < 2 else ckr[:, t, :]
                    nc.tensor.transpose(flat[0:w, at + TP + 128 * t:at + TP + 128 * t + 128], cached, ident[:, :])
                nc.tensor.transpose(flat[0:w, at + TP + PAST:at + NK], nat[0:TS, 4, c0:c0 + w],
                                    ident[0:TS, 0:TS]).then_inc(s_tc, 1)

            def attention(A):
                h_all = A.heads

                def scores(i, s):
                    u, c = s % 5, s // 5
                    if u == 0:
                        need(pe, A.prep_a, c + 1, i, 2)
                        need(pe, A.prep_p, 2 * c + 2, i, 4)
                    need(pe, A.sfree, A.before(s), i, 10)
                    out, nq = A.score(s), A.rows(u)
                    q = slice(128 * u, 128 * u + nq)
                    if A.mem:
                        ks = slice(0, 256) if u < 4 else slice(256, 512)
                        qt, kt = (qmh[:, c, q], qml[:, c, q]), (kmh[:, c, ks], kml[:, c, ks])
                        product(out, None, (qt, kt), True, True).then_inc(A.qk, 1)
                        return
                    ks = slice(0, A.cols(u)) if u < 4 else slice(TP, NK)
                    qt, kt = (qh[:, c, q], ql[:, c, q]), (kh[:, c, ks], kl[:, c, ks])
                    masked = A.name == "fox" or u < 4
                    mm = product(out, None, (qt, kt), True, not masked)
                    if masked:
                        n = nq
                        m = maskb[:, 0 if A.name == "fox" else 1, 0:n]
                        mm = nc.tensor.matmul(out[:, A.cols(u) - n:A.cols(u)], identb[:, 0:n], m, start=False, stop=True)
                    mm.then_inc(A.qk, 1)

                def turn(i, s):
                    u = s % 5
                    need(pe, A.pn, s + 1, i, 10)
                    need(pe, A.ptlo, A.before(s), i, 10)
                    n = A.rows(u) if A.mem else 128
                    for kb in range(A.blocks(u)):
                        mm = nc.tensor.transpose(ps[:, TURN_BANK[u], 128 * kb:128 * kb + n],
                                                 A.p[0:n, u, 128 * kb:128 * kb + 128], ident[0:n, 0:n])
                    mm.then_inc(A.tr, 1)

                def values(i, c):
                    need(pe, A.ptlo, 5 * c + 5, i, 10)
                    need(pe, A.prep_va, c + 1, i, 2)
                    need(pe, A.prep_vp, c + 1, i, 2)
                    need(pe, A.o, c, i, 2)
                    hc = c % 2
                    for kb in range(2 if A.mem else 4):
                        for lo in range(2):
                            t = A.ptlo_t if lo else A.pthi_t
                            if A.mem:
                                rhs, out = t[:, 512 * kb:512 * kb + 512], ps[:, 5, 0:512]
                                mm = nc.tensor.matmul(out, vmh[:, hc, kb, :], rhs, start=(kb == 0 and lo == 0), stop=(kb == 1 and lo == 1))
                                if lo == 0:
                                    nc.tensor.matmul(out, vml[:, hc, kb, :], rhs, start=False, stop=False)
                            else:
                                rhs, out = t[:, 512 * kb:512 * kb + 512 - 128 * kb], ps[:, 5, 128 * kb:512]
                                mm = nc.tensor.matmul(out, vh[:, hc, kb, :], rhs, start=(kb == 0 and lo == 0), stop=(kb == 3 and lo == 1))
                        if kb == (1 if A.mem else 0):
                            mm.then_inc(A.pv0, 1)
                    n = 2 if A.mem else 3
                    at = 1024 if A.mem else 13 * 128
                    for kb in range(n):
                        for lo in range(2):
                            t = A.ptlo_t if lo else A.pthi_t
                            rhs, out = t[:, at + TS * kb:at + TS * kb + TS], ps[:, 6, 0:TS]
                            v = vmh[:, hc, 2 + kb, :] if A.mem else vh[:, hc, 4 + kb, :]
                            mm = nc.tensor.matmul(out, v, rhs, start=(kb == 0 and lo == 0), stop=(kb == n - 1 and lo == 1))
                            if A.mem and lo == 0:
                                nc.tensor.matmul(out, vml[:, hc, 2 + kb, :], rhs, start=False, stop=False)
                    mm.then_inc(A.pv, 1)

                def pair(i, first):
                    for s in range(10):
                        scores(i, s)
                        if not (first and s < 3):
                            turn(i, s - 3)
                        if s % 5 == 4 and not (first and s == 4):
                            values(i, s // 5 - 1)

                pair(0, True)
                if h_all // 2 > 2:
                    with pe.Fori(1, h_all // 2 - 1) as i:
                        pair(i, False)
                pair(h_all // 2 - 1, False)
                turn(h_all // 2, -3)
                turn(h_all // 2, -2)
                turn(h_all // 2, -1)
                values(h_all // 2, -1)

            pe.wait_ge(s_tcev, 7)
            attention(FOX)

            for j in range(4):
                pe.wait_ge(w_lo, B_UQ + j + 1)
                uq_n = 2 * j
                for c in range(2):
                    n = uq_n + c
                    if n >= 2:
                        pe.wait_ge(s_ev, E_UQ + n - 1)
                    if n == 0:
                        pe.wait_ge(s_clo, 5)
                    mm = a_block(B_UQ + j, 3, 0, cqhi, cqlo, n % 2, True, True,
                                 weights=lambda lo, k: wv(B_UQ + j, lo, 3, 256)[:, k, 128 * c:128 * c + 128])
                    if c == 0:
                        mm.then_inc(s_qr, 1)
                    else:
                        mm.then_inc(w_used, 1)
            mean_square("fox")
            for g in range(2):
                b = B_UKV + g
                pe.wait_ge(w_lo, b + 1)
                for q in range(2):
                    n = 2 * g + q
                    pe.wait_ge(s_ev, E_UKV + n - 1)
                    for half in range(2):
                        cols = slice(416 * half, 416 * half + 416)
                        for k in range(2):
                            w = [wv(b, lo, 2, 512)[:, k, 128 * q:128 * q + 128] for lo in range(2)]
                            mm = product(ps[:, 2 * (n % 2) + half, 0:416], b, (w, (ckvhi[:, k, cols], ckvlo[:, k, cols])),
                                         k == 0, k == 1)
                    mm.then_inc(s_qr, 1)
                for t in range(7):
                    m = 7 * g + t
                    rows = 128 if t < 6 else TS
                    if m >= 4:
                        pe.wait_ge(s_vmev, m - 3)
                    elif m == 2:
                        pe.wait_ge(s_std, nth["fox"] + 1)
                    for k in range(2):
                        w = [wv(b, lo, 2, 512)[:, k, 256:512] for lo in range(2)]
                        mm = product(ps[0:rows, 4 + m % 4, 0:256], b,
                                     ((ckvhi[:, k, 128 * t:128 * t + rows], ckvlo[:, k, 128 * t:128 * t + rows]), w),
                                     k == 0, k == 1)
                    mm.then_inc(w_used if t == 6 else s_mt, 1)
            pe.wait_ge(s_ev, E_UKV + 4)
            pe.wait_ge(s_vmev, 14)
            attention(MLA)

            def a_loop(base, e0, n0, xh, xl, kn, iters, mean=None):
                def body(i, first):
                    for c in range(4):
                        need(pe, w_lo, base + c + 1, i, 4)
                        need(pe, s_ev, e0 + c - 1, i, 4)
                        a_block(base + c, kn, 0, xh, xl, c % 2, True, True,
                                n0 if first and c == 0 else None, mean=mean if first and c == 0 else None)\
                            .then_inc(w_used, 1)
                body(0, True)
                if iters > 1:
                    with pe.Fori(1, iters) as i:
                        body(i, False)

            a_loop(B_WO, E_WO, N_OUT, hhi, hlo, KT, 2, mean="mla")
            for kt in range(KT):
                if kt == 0:
                    pe.wait_ge(s_memin, 16 * 3)
                    pe.wait_ge(s_ev, E_WO + 8)
                at = 512 * (kt % 4) + 256 * (kt // 4)
                for t in range(2):
                    mm = nc.tensor.transpose(flat[:, at + 128 * t:at + 128 * t + 128],
                                             memn[:, t, 128 * kt:128 * kt + 128], ident[:, :])
                mm.then_inc(s_kt, 1)
            mean_square("mem")
            for w in range(2):
                for c in range(4):
                    b = B_MKV + 4 * w + c
                    pe.wait_ge(w_lo, b + 1)
                    if w == 0:
                        pe.wait_ge(s_mtl, 2 * c + 2)
                    elif c == 0:
                        pe.wait_ge(s_std, nth["mem"] + 1)
                    b_block(b, 2, 2 * c, 512, (4 + 2 * w, 5 + 2 * w), memT_h, memT_l, tokens, c == 0, c == 3)\
                        .then_inc(w_used, 1)
            a_loop(B_MQ, E_MQ, N_MEM, hhi, hlo, KT, 1)
            pe.wait_ge(s_ev, E_MQ + 4)
            pe.wait_ge(s_mkv, 2)
            for m in range(MH):
                for t in range(4):
                    mm = nc.tensor.transpose(ps[:, m, 128 * t:128 * t + 128], memk[:, t, 128 * m:128 * m + 128], ident[:, :])
                mm.then_inc(s_mkt, 1)
            pe.wait_ge(s_mktev, MH)
            pe.wait_ge(s_mkv, 4)
            attention(MEM)
            pe.wait_ge(MEM.o, MH)
            a_loop(B_MO, E_MO, None, mohi, molo, 4, 2)
            pe.wait_ge(s_ev, E_MO + 8)
            def ffn(i, first):
                for c in range(4):
                    need(pe, w_lo, B_FF + c + 1, i, 4)
                    if c % 2 == 0:
                        need(pe, s_gr, c // 2 - 1, i, 2)
                    else:
                        need(pe, s_hf, c // 2 - 1, i, 2)
                        if first and c == 3:
                            pe.wait_ge(s_std, nth["ffn"] + 1)
                    a_block(B_FF + c, KT, 0, hhi, hlo, c, True, True,
                            N_FFN if first and c == 0 else None).then_inc(w_used, 1)
                    if first and c == 1:
                        mean_square("ffn")

            ffn(0, True)
            with pe.Fori(1, FT // 2) as i:
                ffn(i, False)

            pe.wait_ge(s_hidlo, FT)
            pe.wait_ge(s_gr, FT)
            def down(i, c2):
                k0 = 0
                for c, kn in enumerate(DOWN_K):
                    need(pe, w_lo, B_DOWN + 4 * c2 + c + 1, i, 8)
                    if c == 0:
                        need(pe, s_ev, E_DOWN + c2 - 1, i, 2)
                    a_block(B_DOWN + c, kn, k0, hidhi, hidlo, c2, c == 0, c == 3).then_inc(w_used, 1)
                    k0 += kn

            with pe.Fori(0, 4) as i:
                for c2 in range(2):
                    down(i, c2)
            mean_square("fin")
            for tt in range(TT):
                if tt >= 2:
                    pe.wait_ge(s_yev, tt - 1)
                elif tt == 0:
                    pe.wait_ge(s_yg, KT)
                    pe.wait_ge(s_ev, E_DOWN + 8)
                n = tok(tt)
                for j in range(KT):
                    mm = nc.tensor.transpose(flat[0:n, 1024 * (tt % 2) + 128 * j:1024 * (tt % 2) + 128 * j + 128],
                                             yg[:, j, 128 * tt:128 * tt + n], ident[:, :])
                mm.then_inc(s_yt, 1)
                if tt == 0:
                    pe.wait_ge(s_rstd, nth["fin"] + 1)
                    for t in range(TT):
                        mm = nc.tensor.transpose(ps[0:tok(t), 5, 32 * t:32 * t + 32],
                                                 rstd[0:32, 128 * t:128 * t + tok(t)], ident[0:32, 0:32])
                    mm.then_inc(s_rt, 1)

        @block.scalar
        def _(act):
            copy = ACT.Copy

            def split(c, i=0, per=0):
                act.wait_ge(w_load[c % RAWS], loaded(c) + i * (16 * per // RAWS) if per else loaded(c))
                need(act, w_used, c - SLOTS + 1, i, per)
                nc.scalar.activation(whi[:, c % SLOTS, :], wraw[:, c % RAWS, :], copy).then_inc(w_hi, 1)

            outs = [0]

            def store(dst, src):
                outs[0] += 1
                act.dma_start(dst, src).then_inc(s_out, 16)

            def square(name, j, src, i=0, per=0):
                need(act, s_acc, acc0[name] + j, i, per)
                nc.scalar.activation(tmp2[:, j % 2, :], src, ACT.Square).then_inc(s_sq, 1)

            def std(name, n):
                act.wait_ge(s_ms, nth[name] + 1)
                act.wait_ge(s_const, 1)
                nc.scalar.activation(halves(rstd[:, :]), two(3), ACT.Sqrt, bias=small[:, S_EPS:S_EPS + 1],
                                     scale=1.0 / n).then_inc(s_std, 1)

            def operand(j, n0, src, gain):
                nc.scalar.activation(hhi[:, j, :], src[:, j, :], copy, scale=gains[:, gain + j:gain + j + 1])\
                    .then_inc(s_hhi, 1)

            def prep(A, i, c, parts="qk"):
                p = c % 2
                need(act, A.qk, 5 * c - 5, i, 10)
                pair = i + c // 2
                head = 2 * i + c
                r = slice(64 * p, 64 * p + 64)
                if "q" in parts:
                    if A.mem:
                        nc.scalar.activation(qmh[:, p, :], A.q[:, head, :], copy)
                    elif A.name == "fox":
                        nc.scalar.activation(qh[r, p, :], A.q[r, pair, :], copy)
                    else:
                        nc.scalar.activation(qh[:, p, :], A.q[:, head, :], copy)
                if "k" in parts:
                    if A.mem:
                        nc.scalar.activation(kmh[:, p, :], A.k[:, head, :], copy).then_inc(A.prep_a, 1)
                    else:
                        nc.scalar.activation(kh[r, p, :], A.k[r, pair, :], copy).then_inc(A.prep_a, 1)

            def prep_v(A, i, c):
                p, head = c % 2, 2 * i + c
                need(act, A.pv, c - 1, i, 2)
                if A.mem:
                    nc.scalar.activation(vmh[:, p, :, :], A.v[:, :, bass.ts(head, 128)], copy).then_inc(A.prep_va, 1)
                else:
                    nc.scalar.activation(vh[:, p, :, 0:64], A.v[:, :, bass.ts(head, 64)], copy).then_inc(A.prep_va, 1)

            for n, (dst, src) in enumerate(small_loads):
                act.dma_start(dst, src).then_inc(s_in2, 16)
            act.wait_ge(s_in, 16 * N_IN)
            act.wait_ge(s_acc, 1)
            for j in range(KT):
                act.wait_ge(s_tx, j + 1)
                nc.scalar.activation(xT[:, j, :], flat[:, 1024 * (j % 2):1024 * (j % 2) + T], copy).then_inc(s_x, 1)
                act.wait_ge(s_x, j + 1)
                operand(j, N_MIX, xT, G_MIX)
                if j < SLOTS:
                    split(j)
            for j in range(KT):
                square("mix", j, xT[:, j, :])
            std("mix", D)
            with act.Fori(0, 2) as i:
                for c in range(4):
                    split(B_QK + 4 + c, i, 4)
            for tt in range(TT):
                act.wait_ge(s_kt, tt + 1)
                if tt >= 2:
                    act.wait_ge(s_kdma[tt % 2], 16 * (tt // 2))
                n = tok(tt)
                nc.scalar.activation(kout[0:n, tt % 2, :], ps[0:n, 5 + tt % 2, :], copy).then_inc(s_kout, 1)
                act.wait_ge(s_kout, tt + 1)
                dst = o_["p_fox_k"][128 * tt:128 * tt + 128, :] if tt < 4 else o_["s_fox_k"]
                act.dma_start(dst, kout[0:n, tt % 2, :]).then_inc(s_kdma[tt % 2], 16)
                if tt < 4:
                    split(B_V + 4 + tt)
            act.wait_ge(s_vev, TT)
            store(o_["p_fox_v"].rearrange("(t p) n -> p t n", p=128), vraw[:, 0:4, :])
            store(o_["s_fox_v"], vraw[0:TS, 6, :])
            for c in range(8):
                split(B_TAIL + 4 + c)
            act.wait_ge(s_z, 2)
            nc.scalar.activation(ropt[:, 40:80], ropt[:, 40:80], ACT.Exp).then_inc(s_lnf, 1)
            act.wait_ge(s_lnf, 1)
            nc.scalar.activation(ropt[:, 40:80], ropt[:, 40:80], ACT.Ln, bias=1.0).then_inc(s_lnf, 1)
            act.wait_ge(s_std, 1)
            for tt in range(TT):
                for g, (c0, w) in enumerate(((H, QR), (H + QR, KVR))):
                    nc.scalar.activation(tmp2[:, 0, 0:w], nat[:, tt, c0:c0 + w], ACT.Square,
                                         accum_out=small[:, S_SS + 5 * g + tt:S_SS + 5 * g + tt + 1]).then_inc(s_ss, 1)
                    act.wait_ge(s_ss, 2 * tt + g + 1)
            for g, w in enumerate((QR, KVR)):
                c0 = S_SS + 5 * g
                nc.scalar.activation(small[:, c0:c0 + 5], small[:, c0:c0 + 5], ACT.Sqrt, bias=small[:, S_EPS:S_EPS + 1],
                                     scale=1.0 / w).then_inc(s_sstd, 1)
            act.wait_ge(s_cum, 1)
            act.wait_ge(s_kdma[0], 48)
            act.wait_ge(s_kdma[1], 32)
            nc.scalar.activation(ncum[:, 0:TP], ps[0:8, 5, :], copy, scale=-1.0)
            nc.scalar.activation(ncum[:, TP:NK], ps[0:8, 6, 0:NK - TP], copy, scale=-1.0).then_inc(s_ncum, 1)
            act.wait_ge(s_ncum, 1)
            act.dma_start(cum_dram, ncum[:, :]).then_inc(s_cumd, 16)
            act.wait_ge(s_logf, 1)
            lf = ropt[:, 120:160].rearrange("p (t h) -> p t h", h=H)
            with nc.allow_non_contiguous_dma(reason="rows of 8"):
                store(o_["p_fox_logf"].rearrange("(t p) n -> p t n", p=128), lf[:, 0:4, :])
                store(o_["s_fox_logf"], lf[0:TS, 4, :])
            act.wait_ge(s_tc, 1)
            nc.scalar.activation(kraw[:, :, TP:TP + PAST], flat[:, 0:1024].rearrange("p (h n) -> p h n", h=4), copy)\
                .then_inc(s_tcev, 1)
            act.wait_ge(s_zero, 4)
            act.wait_ge(s_vz, 1)
            act.wait_ge(s_tcev, 1)
            prep(FOX, 0, 0)
            prep_v(FOX, 0, 0)
            for j in range(3):
                act.wait_ge(s_tc, 2 + j)
                at = 1024 * ((j + 1) % 2)
                nc.scalar.activation(cqT[:, j, :], flat[:, at:at + T], copy, scale=gains[:, G_CQ + j:G_CQ + j + 1])\
                    .then_inc(s_tcev, 1)
            for j in range(3):
                act.wait_ge(s_tc, 5 + j)
                at = 1024 * (j % 2)
                if j < 2:
                    nc.scalar.activation(ckvT[:, j, :], flat[:, at:at + NK], copy).then_inc(s_tcev, 1)
                else:
                    nc.scalar.activation(krT[0:RD, :], flat[0:RD, at:at + NK], copy)
                    nc.scalar.activation(krT[64:64 + RD, :], flat[0:RD, at:at + NK], copy).then_inc(s_tcev, 1)
            store(o_["p_mla_ckv"].rearrange("(t p) n -> p t n", p=128), nat[:, 0:4, H + QR:H + QR + KVR])
            store(o_["s_mla_ckv"], nat[0:TS, 4, H + QR:H + QR + KVR])
            store(o_["p_mla_kr"].rearrange("(t p) n -> p t n", p=128), nat[:, 0:4, H + QR + KVR:TAIL_W])
            store(o_["s_mla_kr"], nat[0:TS, 4, H + QR + KVR:TAIL_W])

            def attention(A, prepared=False):
                def expo(i, s):
                    u = s % 5
                    n, w = A.rows(u), A.cols(u)
                    need(act, A.mx, s + 1, i, 10)
                    if A.name != "fox":
                        need(act, A.tr, s - 4, i, 10)
                    src = A.p[0:n, u, 0:w] if A.name == "fox" else A.score(s)
                    nc.scalar.activation(A.p[0:n, u, 0:w], src, ACT.Exp, bias=small[0:n, S_NMAX + u:S_NMAX + u + 1],
                                         scale=-1.0 if A.name == "fox" else 1.0,
                                         accum_out=small[0:n, S_SUM + u:S_SUM + u + 1]).then_inc(A.ex, 1)

                def turned_hi(i, s):
                    u, c = s % 5, s // 5
                    need(act, A.tr, s + 1, i, 10)
                    if u == 0:
                        need(act, A.pv0, c, i, 2)
                    if u == 1:
                        need(act, A.pv, c, i, 2)
                    nc.scalar.activation(A.kept(A.pthi_t, u), A.turned(s), copy).then_inc(A.pthi, 1)

                def out(i, c):
                    need(act, A.pv, c + 1, i, 2)
                    if A.mem:
                        nc.scalar.activation(mohi[:, 2 * i + c, :], flat[:, 5 * 512:5 * 512 + T], copy).then_inc(A.oc, 1)
                        return
                    need(act, A.o, c, i, 2)
                    nc.scalar.activation(osum[:, :], flat[64:128, 5 * 512:5 * 512 + T], copy).then_inc(A.oc, 1)

                def pair(i, first, last):
                    for s in range(10):
                        if s % 5 == 4:
                            expo(i, s)
                        if not (first and s < 4):
                            turned_hi(i, s - 4)
                        if s % 5 < 4:
                            expo(i, s)
                        if s % 5 == 0 and not (last and s == 5):
                            prep(A, i, s // 5 + 1, "q")
                        if s % 5 == 1 and not (last and s == 6):
                            prep(A, i, s // 5 + 1, "k")
                        if s % 5 == 2 and not first:
                            out(i, s // 5 - 2)
                        if s % 5 == 3 and not (first and s == 3):
                            prep_v(A, i, s // 5)

                np_ = A.heads // 2
                if not prepared:
                    prep(A, 0, 0)
                    prep_v(A, 0, 0)
                pair(0, True, False)
                if np_ > 2:
                    with act.Fori(1, np_ - 1) as i:
                        pair(i, False, False)
                pair(np_ - 1, False, True)
                turned_hi(np_, -4)
                out(np_, -2)
                for s in (-3, -2, -1):
                    turned_hi(np_, s)
                out(np_, -1)

            act.wait_ge(s_out, 16 * N_OUT_NAT)
            assert outs[0] == N_OUT_NAT
            act.wait_ge(s_vz, 2)
            attention(FOX, prepared=True)
            for j in range(3):
                nc.scalar.activation(cqhi[:, j, :], cqT[:, j, :], copy).then_inc(s_chi, 1)
            for j in range(2):
                nc.scalar.activation(ckvhi[:, j, :], ckvT[:, j, :], copy).then_inc(s_chi, 1)
            act.wait_ge(s_acc, acc0["fox"] + 1)
            act.wait_ge(FOX.o, H)
            for j in range(4):
                square("fox", j, oT[:, j, :])
            for j in range(4):
                for c in range(2):
                    n = 2 * j + c
                    act.wait_ge(s_qr, j + 1) if c == 0 else act.wait_ge(w_used, B_UQ + j + 1)
                    nc.scalar.activation(halves(qm[:, n, :]), two(n % 2), copy, scale=MLA_SCALE).then_inc(s_qcp, 1)
                split(B_UQ + 4 + j)
            std("fox", 512)
            for g in range(2):
                for t in range(7):
                    act.wait_ge(s_mt, 6 * g + t + 1) if t < 6 else act.wait_ge(w_used, B_UKV + g + 1)
                    rows = 128 if t < 6 else TS
                    nc.scalar.activation(vm[0:rows, t, 256 * g:256 * g + 256], ps[0:rows, 4 + (7 * g + t) % 4, 0:256], copy)\
                        .then_inc(s_vmev, 1)
                split(B_UKV + 4 + g)
                if g == 0:
                    act.wait_ge(s_zero, 6)
                    nc.scalar.activation(kh[64:64 + RD, 0, :], krT[64:64 + RD, :], copy)
                    nc.scalar.activation(kh[0:RD, 1, :], krT[0:RD, :], copy).then_inc(s_krp, 1)
                    act.wait_ge(s_qrope, 1)
                    act.wait_ge(s_ev, E_UKV + 1)
                    prep(MLA, 0, 0)
            act.wait_ge(s_vz, 3)
            act.wait_ge(s_qrope, H)
            act.wait_ge(s_ev, E_UKV + 4)
            act.wait_ge(s_vmev, 14)
            prep_v(MLA, 0, 0)
            attention(MLA, prepared=True)
            act.wait_ge(s_acc, acc0["mla"] + 1)
            act.wait_ge(MLA.o, H)
            for j in range(4):
                act.wait_ge(s_onorm, j + 1)
                nc.scalar.activation(hhi[:, j, :], oT[:, j, :], copy).then_inc(s_hhi, 1)
                square("mla", j, oT[:, 4 + j, :])
            std("mla", 512)
            act.dma_start(memn[:, :, :], i_["mem_prompt"].rearrange("(t p) n -> p t n", p=128)).then_inc(s_memin, 16)
            act.dma_start(memk[:, 2:4, :], i_["cache_mem_k"].rearrange("(t p) n -> p t n", p=128)).then_inc(s_memin, 16)
            act.dma_start(memv[:, 2:4, :], i_["cache_mem_v"].rearrange("(t p) n -> p t n", p=128)).then_inc(s_memin, 16)
            act.wait_ge(w_used, B_UKV + 2)
            for j in range(4, KT):
                act.wait_ge(s_onorm, j + 1)
                nc.scalar.activation(hhi[:, j, :], oT[:, j, :], copy).then_inc(s_hhi, 1)

            def update(name, base, iters, squares=True):
                act.wait_ge(s_acc, acc0[name] + 1)
                with act.Fori(0, iters) as i:
                    for c in range(4):
                        need(act, s_ev, {"mem": E_WO, "ffn": E_MO}[name] + c + 1, i, 4)
                        need(act, s_acc, acc0[name] + c, i, 4)
                        nc.scalar.activation(tmp2[:, c % 2, :], xT[:, 4 * i + c, :], ACT.Square).then_inc(s_sq, 1)
                        split(base + 4 + c, i, 4)

            act.wait_ge(s_memin, 16 * 3)
            act.wait_ge(s_acc, acc0["mla"] + 5)
            junk = tmp2[:, :, :].rearrange("p a b -> p (a b)")[:, 0:D]
            for t in range(2):
                nc.scalar.activation(junk, memn[:, t, :], ACT.Square, accum_out=small[:, S_SS + t:S_SS + t + 1])\
                    .then_inc(s_mss, 1)
                act.wait_ge(s_mss, t + 1)
            nc.scalar.activation(small[:, S_SS:S_SS + 2], small[:, S_SS:S_SS + 2], ACT.Sqrt, bias=small[:, S_EPS:S_EPS + 1],
                                 scale=1.0 / D).then_inc(s_mstd, 1)
            update("mem", B_WO, 2)
            act.wait_ge(s_kt, TT + KT)
            for kt in range(KT):
                if kt >= 4:
                    act.wait_ge(s_mtl, kt - 3)
                at = 512 * (kt % 4) + 256 * (kt // 4)
                nc.scalar.activation(memT_h[:, kt, :], flat[:, at:at + NM], copy, scale=gains[:, G_SRC + kt:G_SRC + kt + 1])\
                    .then_inc(s_mth, 1)
            std("mem", D)
            act.wait_ge(w_used, B_WO + 8)
            for j in range(KT):
                operand(j, N_MEM, xT, G_MEM)
                split(B_MKV + 4 + j)
            act.wait_ge(s_mkv, 4)
            store(o_["p_mem_k"].rearrange("(t p) n -> p t n", p=128), memk[:, 0:2, :])
            store(o_["p_mem_v"].rearrange("(t p) n -> p t n", p=128), memv[:, 0:2, :])
            for c in range(4):
                split(B_MQ + 4 + c)
            for m in range(MH):
                act.wait_ge(s_mkt, m + 1)
                nc.scalar.activation(mkT[:, m, :], ps[:, m, :], copy).then_inc(s_mktev, 1)
            act.wait_ge(s_ev, E_MQ + 4)
            act.wait_ge(s_mktev, MH)
            attention(MEM)
            update("ffn", B_MO, 2)
            for j in range(KT):
                operand(j, N_FFN, xT, G_FFN)
            std("ffn", D)
            act.wait_ge(s_out, 16 * N_OUT_ALL)
            assert outs[0] == N_OUT_ALL
            with act.Fori(0, FT // 2) as i:
                for f in range(2):
                    need(act, s_gr, f + 1, i, 2)
                    nc.scalar.activation(tmp2[:, 0, :], tmp2[:, 0, :], ACT.Silu).then_inc(s_silu, 1)
                    split(B_FF + 4 + 2 * f, i, 4)
                    need(act, s_h2, f + 1, i, 2)
                    nc.scalar.activation(hidhi[:, 2 * i + f, :], tmp2[:, 1, :], copy).then_inc(s_hidhi, 1)
                    split(B_FF + 5 + 2 * f, i, 4)
            act.wait_ge(s_acc, acc0["fin"] + 1)
            act.wait_ge(w_used, B_DOWN)

            def final_tile(i):
                nc.scalar.activation(yg[:, i, :], xT[:, i, :], copy, scale=gains[:, bass.ds(i + G_FIN, 1)])\
                    .then_inc(s_yg, 1)

            with act.Fori(0, 7) as i:
                for c in range(4):
                    split(B_DOWN + 4 + c, i, 4)
                need(act, s_ev, E_DOWN + 1, i, 1)
                need(act, s_acc, acc0["fin"] + 1, i, 1)
                nc.scalar.activation(tmp2[:, 0, :], xT[:, i, :], ACT.Square).then_inc(s_sq, 1)
                final_tile(i)
            act.wait_ge(s_ev, E_DOWN + 8)
            act.wait_ge(s_acc, acc0["fin"] + 8)
            nc.scalar.activation(tmp2[:, 0, :], xT[:, 7, :], ACT.Square).then_inc(s_sq, 1)
            final_tile(7)
            std("fin", D)
            act.wait_ge(s_rcol, 2)
            for tt in range(TT):
                act.wait_ge(s_yt, tt + 1)
                n = tok(tt)
                if tt >= 2:
                    act.wait_ge(s_ydma[tt % 2], 16 * (tt // 2))
                nc.scalar.activation(yout[0:n, tt % 2, :], flat[0:n, 1024 * (tt % 2):1024 * (tt % 2) + D], copy,
                                     scale=rcol[0:n, tt:tt + 1]).then_inc(s_yev, 1)
            act.wait_ge(s_out, 16 * N_OUT_ALL)

        @block.vector
        def _(dve):
            v = nc.vector

            def f(ap):
                return ap.bitcast(F32)

            def start_norm(name):
                need(dve, s_ms, nth[name])
                v.memset(sqacc[:, :], 0.0).then_inc(s_acc, 1)

            def accumulate(name, j, i=0, per=0, slot=None):
                need(dve, s_sq, sq0[name] + j + 1, i, per)
                need(dve, s_acc, acc0[name] + 1 + j, i, per)
                v.tensor_tensor(sqacc[:, :], sqacc[:, :], tmp2[:, j % 2 if slot is None else slot, :], ALU.add)\
                    .then_inc(s_acc, 1)

            def reciprocal_std(name):
                dve.wait_ge(s_std, nth[name] + 1)
                v.reciprocal(rstd[:, :], rstd[:, :]).then_inc(s_rstd, 1)
                dve.wait_ge(s_rstd, nth[name] + 1)

            def operand_lo(j, n0, gain):
                dve.wait_ge(s_hhi, n0 + j + 1)
                v.scalar_tensor_tensor(hlo[:, j, :], xT[:, j, :], gains[:, gain + j:gain + j + 1], f(hhi[:, j, :]),
                                       ALU.mult, ALU.subtract).then_inc(s_hlo, 1)

            v.memset(ones[:, :], 1.0)
            v.memset(small[:, S_EPS:S_EPS + 1], EPS).then_inc(s_const, 1)
            start_norm("mix")
            dve.wait_ge(s_in, 16 * N_IN)
            for j in range(KT):
                operand_lo(j, N_MIX, G_MIX)
            for j in range(KT):
                accumulate("mix", j)
            reciprocal_std("mix")
            for j in range(8):
                dve.wait_ge(w_used, B_QK + j + 1)
                if j < 4:
                    v.scalar_tensor_tensor(halves(qraw[:, j, :]), two(j % 2), FOX_SCALE, halves(rstd[:, :]),
                                           ALU.mult, ALU.mult).then_inc(s_ev, 1)
                else:
                    b, rest = 2 * (j % 2), TP - HT
                    v.tensor_tensor(kraw[:, j - 4, 0:HT], ps[:, b, 0:HT], rstd[:, 0:HT], ALU.mult)
                    v.tensor_tensor(kraw[:, j - 4, HT:TP], ps[:, b + 1, 0:rest], rstd[:, HT:TP], ALU.mult)
                    v.tensor_tensor(kraw[:, j - 4, TP + PAST:NK], ps[:, b + 1, rest:HT], rstd[:, TP:T], ALU.mult)\
                        .then_inc(s_ev, 1)

            def row_factors(bank, nth_):
                dve.wait_ge(s_rt, nth_)
                v.tensor_copy(rcol[:, 0:4], ps[:, bank, 0:128].rearrange("p (t c) -> p t c", c=32)[:, :, 0])
                v.tensor_copy(rcol[0:TS, 4:5], ps[0:TS, bank, 128:129]).then_inc(s_rcol, 1)
                dve.wait_ge(s_rcol, nth_)

            row_factors(7, 1)
            dve.wait_ge(s_tx, KT)
            v.memset(nat[64:128, 4, :], 0.0)
            v.memset(vraw[64:128, 6, :], 0.0).then_inc(s_vz, 1)
            dve.wait_ge(w_used, B_V + 4)
            for tt in range(TT):
                n, t = tok(tt), tt if tt < 4 else 6
                v.tensor_scalar(vraw[0:n, t, :], ps[0:n, tt, :], rcol[0:n, tt:tt + 1], None, ALU.mult).then_inc(s_vev, 1)
            for g in range(2):
                dve.wait_ge(w_used, B_TAIL + 4 * g + 4)
                for tt in range(TT):
                    n = tok(tt)
                    v.tensor_scalar(nat[0:n, tt, TG * g:TG * g + TG], ps[0:n, tt, 0:TG], rcol[0:n, tt:tt + 1], None, ALU.mult)\
                        .then_inc(s_tail, 1)
            dve.wait_ge(s_tail, 2 * TT)
            dve.wait_ge(s_in2, 16 * N_IN2)
            v.tensor_copy(maskb[:, :, :], maskf[:, :, :])
            v.tensor_copy(identb[:, :], ident[:, :])
            z = ropt[:, 0:40].rearrange("p (t h) -> p t h", h=H)
            v.tensor_tensor(z, nat[:, :, 0:H], small[:, S_BF:S_BF + H].unsqueeze(1).to_broadcast([128, TT, H]), ALU.add)\
                .then_inc(s_z, 1)
            dve.wait_ge(s_z, 1)
            v.tensor_scalar(ropt[:, 80:120], ropt[:, 0:40], 0.0, None, ALU.min)
            v.scalar_tensor_tensor(ropt[:, 40:80], ropt[:, 0:40], -1.0, ropt[:, 0:40], ALU.mult, ALU.min).then_inc(s_z, 1)
            dve.wait_ge(s_lnf, 2)
            v.tensor_tensor(ropt[:, 120:160], ropt[:, 80:120], ropt[:, 40:80], ALU.subtract).then_inc(s_logf, 1)
            dve.wait_ge(s_sstd, 2)
            v.reciprocal(small[:, S_SS:S_SS + 10], small[:, S_SS:S_SS + 10]).then_inc(s_srstd, 1)
            dve.wait_ge(s_srstd, 1)
            for tt in range(TT):
                cq = nat[:, tt, H:H + QR]
                mm = v.tensor_scalar(cq, cq, small[:, S_SS + tt:S_SS + tt + 1], None, ALU.mult)
            mm.then_inc(s_natn, 1)
            for tt in range(TT):
                kv = nat[:, tt, H + QR:H + QR + KVR]
                mm = v.scalar_tensor_tensor(kv, kv, small[:, S_SS + 5 + tt:S_SS + 6 + tt], gckv[:, :], ALU.mult, ALU.mult)
            mm.then_inc(s_natn, 1)
            x1, x2 = nat[:, :, TAIL_W - 32:TAIL_W - 16], nat[:, :, TAIL_W - 16:TAIL_W]
            r = [tmp2[:, 1, 80 * k:80 * k + 80].rearrange("p (t c) -> p t c", c=16) for k in range(4)]
            v.tensor_tensor(r[0], x1, cosn[:, :, :], ALU.mult)
            v.tensor_tensor(r[1], x2, sinn[:, :, :], ALU.mult)
            v.tensor_tensor(r[2], x2, cosn[:, :, :], ALU.mult)
            v.tensor_tensor(r[3], x1, sinn[:, :, :], ALU.mult).then_inc(s_kr1, 1)
            dve.wait_ge(s_kr1, 1)
            v.tensor_tensor(x1, r[0], r[1], ALU.subtract)
            v.tensor_tensor(x2, r[2], r[3], ALU.add).then_inc(s_natn, 1)
            dve.wait_ge(s_cumd, 16)
            dve.wait_ge(s_kdma[0], 48)
            dve.wait_ge(s_kdma[1], 32)
            v.memset(probs[64:128, 4, 0:384], 0.0)
            v.memset(probs[0:TS, 4, 320:384], 0.0).then_inc(s_vz, 1)

            def attention(A):
                def maxima(i, s):
                    u, c = s % 5, s // 5
                    n, w = A.rows(u), A.cols(u)
                    need(dve, A.qk, s + 1, i, 10)
                    nmax = small[0:n, S_NMAX + u:S_NMAX + u + 1]
                    if A.name == "fox":
                        if u == 0:
                            need(dve, s_nck[c], 16, i, 16)
                        need(dve, A.tr, s - 4, i, 10)
                        at = 0 if u < 4 else TP
                        if not isinstance(i, int):
                            v.memset(small[:, S_WAIT + u:S_WAIT + u + 1], 0.0)
                        v.tensor_tensor_reduce(A.p[0:n, u, 0:w], A.score(s), nck[0:n, c, at:at + w], -1.0, BIG,
                                               ALU.add, ALU.min, nmax).then_inc(A.mx, 1)
                    else:
                        need(dve, A.ex, s - 4, i, 10)
                        v.tensor_reduce(nmax, A.score(s), AX, ALU.max, negate=True).then_inc(A.mx, 1)

                def normalise(i, s):
                    u = s % 5
                    n, w = A.rows(u), A.cols(u)
                    need(dve, A.ex, s + 1, i, 10)
                    rinv = small[0:n, S_RINV + u:S_RINV + u + 1]
                    v.reciprocal(rinv, small[0:n, S_SUM + u:S_SUM + u + 1]).then_inc(A.ri, 1)
                    need(dve, A.ri, s + 1, i, 10)
                    p = A.p[0:n, u, 0:w]
                    v.tensor_scalar(p, p, rinv, None, ALU.mult).then_inc(A.pn, 1)

                def turned_lo(i, s):
                    u = s % 5
                    need(dve, A.pthi, s + 1, i, 10)
                    v.tensor_tensor(A.kept(A.ptlo_t, u), A.turned(s), f(A.kept(A.pthi_t, u)), ALU.subtract)\
                        .then_inc(A.ptlo, 1)

                def out(i, c):
                    need(dve, A.oc, c + 1, i, 2)
                    o = flat[:, 5 * 512:5 * 512 + T]
                    if A.mem:
                        v.tensor_tensor(molo[:, 2 * i + c, :], o, f(mohi[:, 2 * i + c, :]), ALU.subtract).then_inc(A.o, 1)
                        return
                    p = c % 2
                    v.tensor_tensor(oT[64 * p:64 * p + 64, A.o0 + (i - 1 if c < 0 else i), :], o[0:64], osum[:, :], ALU.add)\
                        .then_inc(A.o, 1)

                def pair(i, first):
                    for s in range(10):
                        if not (first and s < 5):
                            turned_lo(i, s - 5)
                        maxima(i, s)
                        if not (first and s < 1):
                            normalise(i, s - 1)
                        if s % 5 == 2 and not first:
                            out(i, s // 5 - 2)

                np_ = A.heads // 2
                pair(0, True)
                if np_ > 2:
                    with dve.Fori(1, np_ - 1) as i:
                        pair(i, False)
                pair(np_ - 1, False)
                normalise(np_, -1)
                out(np_, -2)
                for s in range(-5, 0):
                    turned_lo(np_, s)
                out(np_, -1)
                dve.wait_ge(A.o, A.heads)

            dve.wait_ge(s_out, 16 * N_OUT_NAT)
            attention(FOX)
            start_norm("fox")
            for j in range(3):
                dve.wait_ge(s_chi, j + 1)
                v.tensor_tensor(cqlo[:, j, :], cqT[:, j, :], f(cqhi[:, j, :]), ALU.subtract).then_inc(s_clo, 1)
            for j in range(2):
                dve.wait_ge(s_chi, 3 + j + 1)
                v.tensor_tensor(ckvlo[:, j, :], ckvT[:, j, :], f(ckvhi[:, j, :]), ALU.subtract).then_inc(s_clo, 1)
            for j in range(4):
                accumulate("fox", j)
            dve.wait_ge(s_acc, acc0["fox"] + 5)
            for n in range(8):
                dve.wait_ge(s_qcp, n + 1)
                r0 = 64 if n % 2 == 0 else 0
                a, b = slice(r0, r0 + 32), slice(r0 + 32, r0 + 64)
                pr = two(n % 2)
                v.tensor_tensor(halves(tmp2[a, 1, :]), pr[b], halves(rope[b, :]), ALU.mult)
                v.tensor_tensor(halves(qm[a, n, :]), pr[a], halves(rope[a, :]), ALU.mult).then_inc(s_ev, 1)
                dve.wait_ge(s_ev, E_UQ + n + 1)
                v.tensor_tensor(qm[a, n, :], qm[a, n, :], tmp2[a, 1, :], ALU.add).then_inc(s_qrope, 1)
            v.memset(vm[64:128, 6, :], 0.0).then_inc(s_vz, 1)
            for n in range(4):
                dve.wait_ge(s_qr, 4 + n + 1)
                b = 2 * (n % 2)
                v.tensor_copy(km[:, n, :].rearrange("p (a b) -> p a b", a=2), ps[:, b:b + 2, 0:416]).then_inc(s_ev, 1)
            reciprocal_std("fox")
            for j in range(4):
                v.scalar_tensor_tensor(oT[:, j, :], oT[:, j, :], gains[:, G_OUT + j:G_OUT + j + 1], rstd[:, :],
                                       ALU.mult, ALU.mult).then_inc(s_onorm, 1)
            attention(MLA)
            def mixed_lo(j):
                dve.wait_ge(s_hhi, N_OUT + j + 1)
                v.tensor_tensor(hlo[:, j, :], oT[:, j, :], f(hhi[:, j, :]), ALU.subtract).then_inc(s_hlo, 1)

            start_norm("mla")
            for j in range(4):
                mixed_lo(j)
                accumulate("mla", j)
            reciprocal_std("mla")
            for j in range(4):
                v.scalar_tensor_tensor(oT[:, 4 + j, :], oT[:, 4 + j, :], gains[:, G_OUT + 4 + j:G_OUT + 5 + j],
                                       rstd[:, :], ALU.mult, ALU.mult).then_inc(s_onorm, 1)
            for j in range(4, KT):
                mixed_lo(j)

            def update(name, base):
                start_norm(name)
                with dve.Fori(0, 2) as i:
                    for c in range(4):
                        need(dve, w_used, base + c + 1, i, 4)
                        x = xT[:, 4 * i + c, :]
                        v.tensor_tensor(halves(x), two(c % 2), halves(x), ALU.add).then_inc(s_ev, 1)
                        accumulate(name, c, i, 4)

            update("mem", B_WO)
            dve.wait_ge(s_mstd, 1)
            v.reciprocal(rcol[:, 5:7], small[:, S_SS:S_SS + 2]).then_inc(s_mrstd, 1)
            for kt in range(KT):
                dve.wait_ge(s_mth, kt + 1)
                at = 512 * (kt % 4) + 256 * (kt // 4)
                v.scalar_tensor_tensor(memT_l[:, kt, :], flat[:, at:at + NM], gains[:, G_SRC + kt:G_SRC + kt + 1],
                                       f(memT_h[:, kt, :]), ALU.mult, ALU.subtract).then_inc(s_mtl, 1)
            for j in range(KT):
                operand_lo(j, N_MEM, G_MEM)
            reciprocal_std("mem")
            dve.wait_ge(s_mrstd, 1)
            for w, t_ in enumerate((memk, memv)):
                dve.wait_ge(w_used, B_MKV + 4 * w + 4)
                for t in range(2):
                    v.tensor_scalar(t_[:, t, :], ps[:, 4 + 2 * w + t, :], rcol[:, 5 + t:6 + t], None, ALU.mult).then_inc(s_mkv, 1)
            for j in range(4):
                dve.wait_ge(w_used, B_MQ + j + 1)
                v.scalar_tensor_tensor(halves(mqT[:, j, :]), two(j % 2), MEM_SCALE, halves(rstd[:, :]), ALU.mult, ALU.mult)\
                    .then_inc(s_ev, 1)
            attention(MEM)
            update("ffn", B_MO)
            for j in range(KT):
                operand_lo(j, N_FFN, G_FFN)
            reciprocal_std("ffn")
            dve.wait_ge(s_out, 16 * N_OUT_ALL)
            with dve.Fori(0, FT // 2) as i:
                for t in range(2):
                    need(dve, w_used, B_FF + 2 * t + 1, i, 4)
                    v.tensor_tensor(halves(tmp2[:, 0, :]), two(2 * t), halves(rstd[:, :]), ALU.mult).then_inc(s_gr, 1)
                    need(dve, w_used, B_FF + 2 * t + 2, i, 4)
                    need(dve, s_hidlo, t, i, 2)
                    v.tensor_tensor(halves(tmp2[:, 1, :]), two(2 * t + 1), halves(rstd[:, :]), ALU.mult).then_inc(s_hf, 1)
                    need(dve, s_hf, t + 1, i, 2)
                    need(dve, s_silu, t + 1, i, 2)
                    v.tensor_tensor(tmp2[:, 1, :], tmp2[:, 1, :], tmp2[:, 0, :], ALU.mult).then_inc(s_h2, 1)
                    need(dve, s_h2, t + 1, i, 2)
                    need(dve, s_hidhi, t + 1, i, 2)
                    v.tensor_tensor(hidlo[:, 2 * i + t, :], tmp2[:, 1, :], f(hidhi[:, 2 * i + t, :]), ALU.subtract)\
                        .then_inc(s_hidlo, 1)
            start_norm("fin")

            def last_update(i, c):
                need(dve, w_used, B_DOWN + 4 * c + 4, i, 8)
                x = xT[:, 2 * i + c, :]
                v.tensor_tensor(halves(x), two(c), halves(x), ALU.add).then_inc(s_ev, 1)
                accumulate("fin", c, i, 2, slot=0)

            with dve.Fori(0, 4) as i:
                for c in range(2):
                    last_update(i, c)
            reciprocal_std("fin")
            row_factors(5, 2)

        @block.gpsimd
        def _(pool):
            g = nc.gpsimd

            def rest(c, i=0, per=0):
                need(pool, w_hi, c + 1, i, per)
                g.tensor_tensor(wlo[:, c % SLOTS, :], wraw[:, c % RAWS, :], whi[:, c % SLOTS, :].bitcast(F32),
                                ALU.subtract).then_inc(w_lo, 1)

            def rests(first, count):
                with pool.Fori(0, count // 4) as i:
                    for c in range(4):
                        rest(first + c, i, 4)

            def preps(A):
                def prep(i, c):
                    p, head, pair = c % 2, 2 * i + c, i + c // 2
                    r = slice(64 * p, 64 * p + 64)
                    if A.mem:
                        q, k = (qml[:, p, :], A.q[:, head, :], qmh[:, p, :]), (kml[:, p, :], A.k[:, head, :], kmh[:, p, :])
                    else:
                        rq = r if A.name == "fox" else slice(0, 128)
                        q = (ql[rq, p, :], A.q[rq, pair if A.name == "fox" else head, :], qh[rq, p, :])
                        k = (kl[r, p, :], A.k[r, pair, :], kh[r, p, :])
                    need(pool, A.prep_vp, c - 1, i, 2)
                    need(pool, A.prep_p, 2 * c, i, 4)
                    need(pool, A.prep_a, c + 1, i, 2)
                    g.tensor_tensor(q[0], q[1], q[2].bitcast(F32), ALU.subtract).then_inc(A.prep_p, 1)
                    need(pool, A.prep_p, 2 * c + 1, i, 4)
                    g.tensor_tensor(k[0], k[1], k[2].bitcast(F32), ALU.subtract).then_inc(A.prep_p, 1)

                def prep_v(i, p, last=False):
                    head = 2 * i + p
                    if A.mem:
                        vl, vv, vhi = vml[:, p, :, :], A.v[:, :, bass.ts(head, 128)], vmh[:, p, :, :]
                    else:
                        vl, vv, vhi = vh[:, p, :, 64:128], A.v[:, :, bass.ts(head, 64)], vh[:, p, :, 0:64]
                    need(pool, A.prep_p, 2 * p + (2 if last else 4), i, 4)
                    need(pool, A.prep_va, p + 1, i, 2)
                    g.tensor_tensor(vl, vv, vhi.bitcast(F32), ALU.subtract).then_inc(A.prep_vp, 1)

                def pair(i, last=False):
                    for p in range(2):
                        if not (last and p == 1):
                            prep(i, p + 1)
                        prep_v(i, p, last and p == 1)

                prep(0, 0)
                pair(0)
                if A.heads // 2 > 2:
                    with pool.Fori(1, A.heads // 2 - 1) as i:
                        pair(i)
                pair(A.heads // 2 - 1, last=True)

            rests(0, B_UKV)
            pool.wait_ge(w_used, B_UQ)
            for t in (qh, ql, kh, kl):
                g.memset(t[:, :, :].bitcast(F32), 0.0).then_inc(s_zero, 1)
            preps(FOX)
            for b in range(B_UKV, B_WO + 2):
                rest(b)
            pool.wait_ge(w_used, B_UKV)
            for t in (kh, kl):
                g.memset(t[:, :, :].bitcast(F32), 0.0).then_inc(s_zero, 1)
            pool.wait_ge(s_krp, 1)
            g.tensor_tensor(kl[64:64 + RD, 0, :], krT[64:64 + RD, :], kh[64:64 + RD, 0, :].bitcast(F32), ALU.subtract)\
                .then_inc(s_krl, 1)
            pool.wait_ge(s_krl, 1)
            g.tensor_tensor(kl[0:RD, 1, :], krT[0:RD, :], kh[0:RD, 1, :].bitcast(F32), ALU.subtract)\
                .then_inc(s_krl, 1)
            pool.wait_ge(s_krl, 2)
            preps(MLA)
            rest(B_WO + 2)
            rest(B_WO + 3)
            rests(B_WO + 4, B_MO + 4 - (B_WO + 4))
            preps(MEM)
            rests(B_MO + 4, B_END - (B_MO + 4))

        @block.sync
        def _(sp):
            def slot(c, k=None, n=None):
                r = wraw[:, c % RAWS, 0:k * n]
                return r.rearrange("p (k n) -> p k n", k=k)

            def load(c, src, i=0, per=0):
                need(sp, w_lo, c - RAWS + 1, i, per)
                k, n = src.shape[0] // 128, src.shape[1]
                sp.dma_start(slot(c, k, n), src.rearrange("(k p) n -> p k n", p=128)).then_inc(w_load[c % RAWS], 16)

            for dst, src in first_loads[0:3]:
                sp.dma_start(dst, src).then_inc(s_in, 16)
            with nc.allow_non_contiguous_dma(reason="gains onto partitions"):
                for dst, src in first_loads[3:]:
                    sp.dma_start(dst, src).then_inc(s_in, 16)

            def columns(w, first, last, base):
                for i0 in ([0] if first == 0 else []):
                    for c in range(4):
                        load(base + c, w[:, 128 * c:128 * c + 128])
                with sp.Fori(max(first, 1), last) as i:
                    for c in range(4):
                        load(base + c, w[:, bass.ds(512 * i + 128 * c, 128)], i, 4)

            def rows(w, c0, width, base):
                for c in range(4):
                    load(base + c, w[256 * c:256 * c + 256, c0:c0 + width])

            columns(i_["w_in"], 0, 2, B_QK)
            rows(i_["w_in"], 2 * H * HD, 512, B_V)
            rows(i_["w_in"], TAIL0, TG, B_TAIL)
            rows(i_["w_in"], TAIL0 + TG, TG, B_TAIL + 4)
            for j in range(4):
                b = B_UQ + j
                sp.wait_ge(w_lo, b - RAWS + 1)
                dst = slot(b, 3, 256)
                w = i_["w_uq"].rearrange("(k p) n -> p k n", p=128)
                even, odd = 192 * j, 192 * j + 96
                for to, of, n in ((0, even, 96), (96, even + 80, 16), (112, even + 64, 16),
                                  (128, odd + 64, 32), (160, odd + 80, 16), (176, odd + 64, 16), (192, odd, 64)):
                    sp.dma_start(dst[:, :, to:to + n], w[:, :, of:of + n]).then_inc(w_load[b % RAWS], 16)
            sp.wait_ge(s_cumd, 16)
            sp.wait_ge(w_used, B_UQ)
            for c in range(2):
                sp.dma_start(nck[:, c, :], cum_dram[c:c + 1, :].to_broadcast([128, NK])).then_inc(s_nck[c], 16)
            with sp.Fori(1, H // 2) as i:
                for c in range(2):
                    need(sp, FOX.mx, 5 * c - 5, i, 10)
                    sp.dma_start(nck[:, c, :], cum_dram[bass.ds(2 * i + c, 1), :].to_broadcast([128, NK]))\
                        .then_inc(s_nck[c], 16)
            for g in range(2):
                b = B_UKV + g
                sp.wait_ge(w_lo, b - RAWS + 1)
                w = i_["w_ukv"].rearrange("(k p) (h e) -> p k h e", p=128, e=128)
                for k in range(2):
                    for part in range(2):
                        sp.dma_start(slot(b, 2, 512)[:, k, 256 * part:256 * part + 256].rearrange("p (h e) -> p h e", e=64),
                                     w[:, k, 4 * g:4 * g + 4, 64 * part:64 * part + 64]).then_inc(w_load[b % RAWS], 16)
            columns(i_["w_o"], 0, 2, B_WO)
            rows(i_["w_mk"], 0, 512, B_MKV)
            rows(i_["w_mv"], 0, 512, B_MKV + 4)
            for c in range(4):
                load(B_MQ + c, i_["w_mq"][:, 128 * c:128 * c + 128])
            columns(i_["w_mo"], 0, 2, B_MO)
            with sp.Fori(0, FT // 2) as i:
                for c in range(4):
                    load(B_FF + c, i_["w_up" if c % 2 else "w_gate"][:, bass.ds(256 * i + 128 * (c // 2), 128)], i, 4)
            with sp.Fori(0, KT) as i:
                k0 = 0
                for c, kn in enumerate(DOWN_K):
                    load(B_DOWN + c, i_["w_down"][128 * k0:128 * (k0 + kn), bass.ds(128 * i, 128)], i, 4)
                    k0 += kn
            for tt in range(TT):
                sp.wait_ge(s_yev, tt + 1)
                n = tok(tt)
                dst = o_["y_prompt"][128 * tt:128 * tt + 128, :] if tt < 4 else o_["y_sample"]
                sp.dma_start(dst, yout[0:n, tt % 2, :]).then_inc(s_ydma[tt % 2], 16)
            sp.wait_ge(s_ydma[0], 48)
            sp.wait_ge(s_ydma[1], 32)


def constants():
    c = np.zeros((128, C_END), np.float32)
    r = np.arange(128)
    c[:, C_ID:C_ID + 128] = np.eye(128, dtype=np.float32)
    c[:, C_CAUSAL:C_CAUSAL + 128] = np.where(r[None, :] <= r[:, None], 0.0, MASKED)
    c[:, C_CHUNK:C_CHUNK + 128] = np.where(r[None, :] // 64 <= r[:, None] // 64, 0.0, MASKED)
    c[:, C_TRI:C_TRI + 512] = 1.0
    c[:, C_TRI:C_TRI + 128] = np.where(r[:, None] <= r[None, :], 1.0, 0.0)
    half = RD // 2
    inv = np.float32(10000.0) ** (-np.arange(half, dtype=np.float32) / np.float32(half))
    pos = np.concatenate([np.arange(TP), PAST + np.arange(TS)]).astype(np.float32)
    ang = pos[:, None] * inv[None, :]
    cos, sin = np.cos(ang).astype(np.float32), np.sin(ang).astype(np.float32)
    sc = np.float32(MLA_SCALE)
    for r0 in (0, 64):
        c[r0:r0 + 32, C_ROPE:C_ROPE + T] = np.concatenate([cos, cos], 1).T * sc
        c[r0 + 32:r0 + 64, C_ROPE:C_ROPE + T] = np.concatenate([-sin, sin], 1).T * sc
    for tt in range(TT):
        n = tok(tt)
        c[0:n, C_COS + 16 * tt:C_COS + 16 * tt + 16] = cos[128 * tt:128 * tt + n]
        c[0:n, C_SIN + 16 * tt:C_SIN + 16 * tt + 16] = sin[128 * tt:128 * tt + n]
    return c


def kernel(x_prompt, x_sample, mem_prompt, cache_fox_k, cache_fox_v, cache_fox_logf, cache_mla_ckv, cache_mla_kr,
           cache_mem_k, cache_mem_v, g_mix, w_in, b_f, g_cq, w_uq, g_ckv, w_ukv, g_fox_out, g_mla_out, w_o,
           g_mem_src, w_mk, w_mv, g_mem, w_mq, w_mo, g_ffn, w_gate, w_up, w_down, g_final):
    import concourse.bacc as bacc
    from concourse.bass_utils import run_bass_kernel_spmd

    arrays = dict(
        x_prompt=x_prompt, x_sample=x_sample, mem_prompt=mem_prompt, cache_fox_k=cache_fox_k, cache_fox_v=cache_fox_v,
        cache_fox_logf=cache_fox_logf, cache_mla_ckv=cache_mla_ckv, cache_mla_kr=cache_mla_kr, cache_mem_k=cache_mem_k,
        cache_mem_v=cache_mem_v, g_mix=g_mix, w_in=w_in, b_f=b_f, g_cq=g_cq, w_uq=w_uq, g_ckv=g_ckv, w_ukv=w_ukv,
        g_fox_out=g_fox_out, g_mla_out=g_mla_out, w_o=w_o, g_mem_src=g_mem_src, w_mk=w_mk, w_mv=w_mv, g_mem=g_mem,
        w_mq=w_mq, w_mo=w_mo, g_ffn=g_ffn, w_gate=w_gate, w_up=w_up, w_down=w_down, g_final=g_final)
    rows = dict(x_prompt=TP, x_sample=TS, mem_prompt=NM, cache_fox_k=PAST, cache_fox_v=PAST, cache_fox_logf=PAST,
                cache_mla_ckv=PAST, cache_mla_kr=PAST, cache_mem_k=NM, cache_mem_v=NM, b_f=1, g_ckv=1, w_in=D, w_uq=QR,
                w_ukv=KVR, w_o=D, w_mk=D, w_mv=D, w_mq=D, w_mo=MH * MD, w_gate=D, w_up=D, w_down=FF)
    arrays = {k: np.ascontiguousarray(a) for k, a in arrays.items()}
    ins = {k: a.reshape(rows.get(k, a.size), -1) for k, a in arrays.items()}
    ins["consts"] = constants()
    outs = dict(y_prompt=(TP, D), y_sample=(TS, D), p_fox_k=(TP, 512), p_fox_v=(TP, 512), p_fox_logf=(TP, H),
                p_mla_ckv=(TP, KVR), p_mla_kr=(TP, RD), p_mem_k=(NM, 512), p_mem_v=(NM, 512), s_fox_k=(TS, 512),
                s_fox_v=(TS, 512), s_fox_logf=(TS, H), s_mla_ckv=(TS, KVR), s_mla_kr=(TS, RD))
    nc = bacc.Bacc("TRN2", target_bir_lowering=False, num_devices=1)
    i_ = {k: nc.dram_tensor(k, a.shape, F32, kind="ExternalInput").ap() for k, a in ins.items()}
    o_ = {k: nc.dram_tensor("out_" + k, shape, F32, kind="ExternalOutput").ap() for k, shape in outs.items()}
    cum = nc.dram_tensor("gate_sums", (H, NK), F32, kind="Internal").ap()
    build(nc, i_, o_, cum)
    r = run_bass_kernel_spmd(nc, [ins], core_ids=[0]).results[0]
    heads = dict(p_fox_k=(H, HD), p_fox_v=(H, HD), s_fox_k=(H, HD), s_fox_v=(H, HD), p_mem_k=(MH, MD), p_mem_v=(MH, MD))
    got = []
    for k, (n, w) in outs.items():
        a = r["out_" + k]
        if k in ("y_prompt", "y_sample"):
            got.append(a.reshape(1, n, w))
        else:
            got.append(a.reshape((1, 1, n) + heads.get(k, (w,))))
    return tuple(got)
```
